# Optimizing a Trainium2 kernel written in Bass

```python
import jax, jax.numpy as jnp
from jax import lax
import numpy as np

D_MODEL = 1024
BATCH = 1
SEQ = 512
DEPTH = 2

HEAD_DIM = 64
N_HEADS = D_MODEL // HEAD_DIM
N_A = max(1, DEPTH // 2)
N_B = DEPTH - N_A
DECAY_LORA = 64
AAA_LORA = 64
MV_LORA = 32
GATE_LORA = 160
N_GROUPS = 4
EXP_PER_GROUP = 8
N_EXPERTS = N_GROUPS * EXP_PER_GROUP
TOP_K = 2
D_EXPERT = 512
EXPERT_BLOCK = 128
Q_BLOCK = 128
DEEPNORM_ALPHA = (2 * DEPTH) ** 0.25
DEEPNORM_BETA = (8 * DEPTH) ** -0.25
LN_EPS = 1e-5
GN_EPS = 64e-5
QK_EPS = 1e-6


def layer_norm(x, g, b, eps=LN_EPS):
    xf = x.astype(jnp.float32)
    mu = xf.mean(-1, keepdims=True)
    var = jnp.square(xf - mu).mean(-1, keepdims=True)
    return ((xf - mu) * lax.rsqrt(var + eps)).astype(x.dtype) * g + b

def head_rms(t, g, eps=QK_EPS):
    tf = t.astype(jnp.float32)
    return (tf * lax.rsqrt(jnp.mean(tf * tf, -1, keepdims=True) + eps)).astype(t.dtype) * g

def wkv7_scan(r, w, k, v, a, b):
    B, S, H, N = r.shape

    def step(state, inp):
        r_t, w_t, k_t, v_t, a_t, b_t = inp
        sa = jnp.einsum('bhij,bhj->bhi', state, a_t)
        state = (state * w_t[:, :, None, :] + sa[..., None] * b_t[:, :, None, :]
                 + v_t[..., None] * k_t[:, :, None, :])
        return state, jnp.einsum('bhij,bhj->bhi', state, r_t)

    tm = lambda t: jnp.moveaxis(t, 1, 0)
    state0 = jnp.zeros((B, H, N, N), jnp.float32)
    _, y = lax.scan(step, state0, (tm(r), tm(w), tm(k), tm(v), tm(a), tm(b)))
    return jnp.moveaxis(y, 0, 1)

def rwkv7_time_mix(h, v_first, mu, w_rkv, w0, w1, w2, a0, a1, a2, g1, g2,
                   k_k, k_a, r_k, gn_g, gn_b, w_o, v_mix):
    B, S, D = h.shape
    f32 = jnp.float32
    xx = jnp.pad(h, ((0, 0), (1, 0), (0, 0)))[:, :-1] - h
    xr, xw, xk, xv, xa, xg = [h + xx * mu[i] for i in range(6)]
    r, k, v = jnp.einsum('nbsd,nde->nbse', jnp.stack([xr, xk, xv]), w_rkv)
    w_log = -jnp.exp((-jax.nn.softplus(-(w0 + jnp.tanh(xw @ w1) @ w2)) - 0.5).astype(f32))
    if v_mix is None:
        v_first = v
    else:
        v0, v1, v2 = v_mix
        v = v + (v_first - v) * jax.nn.sigmoid(v0 + (xv @ v1) @ v2)
    a = jax.nn.sigmoid(a0 + (xa @ a1) @ a2)
    g = jax.nn.sigmoid(xg @ g1) @ g2
    heads = lambda t: t.reshape(B, S, N_HEADS, HEAD_DIM).astype(f32)
    kk = heads(k * k_k)
    kk = kk / jnp.maximum(jnp.sqrt(jnp.sum(kk * kk, -1, keepdims=True)), 1e-12)
    k = k * (1 + (a - 1) * k_a)
    rh, kh, vh, ah = heads(r), heads(k), heads(v), heads(a)
    y = wkv7_scan(rh, jnp.exp(heads(w_log)), kh, vh, -kk, kk * ah)
    ym = y.mean(-1, keepdims=True)
    yv = jnp.square(y - ym).mean(-1, keepdims=True)
    y = ((y - ym) * lax.rsqrt(yv + GN_EPS)).reshape(B, S, D).astype(h.dtype) * gn_g + gn_b
    bonus = (jnp.sum(rh * kh * r_k, -1, keepdims=True) * vh).reshape(B, S, D).astype(h.dtype)
    return ((y + bonus) * g) @ w_o, v_first

def shared_kv(x, cs, ada_w, ada_b, w_kvf, b_f, k_norm):
    B, S, D = x.shape
    shift, scale = jnp.split(cs @ ada_w + ada_b, 2, axis=-1)
    hk = x * (1 + scale[:, None]) + shift[:, None]
    kvf = hk @ w_kvf
    k = head_rms(kvf[..., :D].reshape(B, S, N_HEADS, HEAD_DIM), k_norm)
    v = kvf[..., D:2 * D].reshape(B, S, N_HEADS, HEAD_DIM)
    log_f = jax.nn.log_sigmoid((kvf[..., 2 * D:] + b_f).astype(jnp.float32))
    fcum = jnp.cumsum(log_f, axis=1)
    return (k.transpose(0, 2, 1, 3), v.transpose(0, 2, 1, 3), fcum.transpose(0, 2, 1))

def forgetting_attention(q, k, v, fcum):
    S = q.shape[2]
    scale = HEAD_DIM ** -0.5
    outs = []
    for i in range(S // Q_BLOCK):
        lo, hi = i * Q_BLOCK, (i + 1) * Q_BLOCK
        logits = (jnp.einsum('bhqd,bhkd->bhqk', q[:, :, lo:hi], k[:, :, :hi]).astype(jnp.float32) * scale
                  + (fcum[:, :, lo:hi, None] - fcum[:, :, None, :hi]))
        causal = (lo + jnp.arange(Q_BLOCK))[:, None] >= jnp.arange(hi)[None, :]
        logits = jnp.where(causal, logits, -jnp.inf)
        p = jax.nn.softmax(logits, axis=-1).astype(v.dtype)
        outs.append(jnp.einsum('bhqk,bhkd->bhqd', p, v[:, :, :hi]))
    return jnp.concatenate(outs, axis=2)

def fox_layer(h, kv, w_qg, q_norm, w_o):
    B, S, D = h.shape
    k, v, fcum = kv
    qg = h @ w_qg
    q = head_rms(qg[..., :D].reshape(B, S, N_HEADS, HEAD_DIM), q_norm).transpose(0, 2, 1, 3)
    o = forgetting_attention(q, k, v, fcum).transpose(0, 2, 1, 3).reshape(B, S, D)
    return (o * jax.nn.sigmoid(qg[..., D:])) @ w_o

def grouped_experts(xf, expert_idx, gates, w_gate, w_up, w_down):
    T, D = xf.shape
    A = T * TOP_K
    n_blocks = -(-(A + N_EXPERTS * EXPERT_BLOCK) // EXPERT_BLOCK)
    n_slots = n_blocks * EXPERT_BLOCK
    flat_e = expert_idx.reshape(A)
    order = jnp.argsort(flat_e)
    sorted_e = flat_e[order]
    counts = jnp.bincount(flat_e, length=N_EXPERTS)
    padded = (counts + EXPERT_BLOCK - 1) // EXPERT_BLOCK * EXPERT_BLOCK
    pad_end = jnp.cumsum(padded)
    pad_start = pad_end - padded
    start = jnp.cumsum(counts) - counts
    dest_sorted = pad_start[sorted_e] + (jnp.arange(A) - start[sorted_e])
    dest = jnp.zeros((A,), jnp.int32).at[order].set(dest_sorted.astype(jnp.int32))
    slot_tok = jnp.zeros((n_slots,), jnp.int32).at[dest].set(jnp.arange(A, dtype=jnp.int32) // TOP_K)
    block_exp = jnp.minimum(jnp.searchsorted(pad_end, jnp.arange(n_blocks) * EXPERT_BLOCK, side='right'),
                            N_EXPERTS - 1)
    xs = xf[slot_tok].reshape(n_blocks, EXPERT_BLOCK, D)

    def one_block(args):
        xb, e = args
        hb = jax.nn.silu(xb @ w_gate[e]) * (xb @ w_up[e])
        return hb @ w_down[e]

    ys = lax.map(one_block, (xs, block_exp)).reshape(n_slots, D)
    y_assign = ys[dest].reshape(T, TOP_K, D)
    return jnp.einsum('tk,tkd->td', gates, y_assign)

def hier_moe(h, w_grp, b_grp, w_exp, b_exp, w_gate, w_up, w_down):
    B, S, D = h.shape
    T = B * S
    hf = h.reshape(T, D)
    p_grp = jax.nn.softmax((hf @ w_grp).astype(jnp.float32) + b_grp, axis=-1)
    g_sel = jnp.argmax(p_grp, axis=-1)
    p_g = jnp.take_along_axis(p_grp, g_sel[:, None], axis=-1)
    e_logits = ((hf @ w_exp).astype(jnp.float32) + b_exp).reshape(T, N_GROUPS, EXP_PER_GROUP)
    e_logits = jnp.take_along_axis(e_logits, g_sel[:, None, None], axis=1)[:, 0]
    top_p, top_i = lax.top_k(jax.nn.softmax(e_logits, axis=-1), TOP_K)
    gates = (p_g * top_p / jnp.sum(top_p, -1, keepdims=True)).astype(h.dtype)
    expert_idx = (g_sel[:, None] * EXP_PER_GROUP + top_i).astype(jnp.int32)
    return grouped_experts(hf, expert_idx, gates, w_gate, w_up, w_down).reshape(B, S, D)

def first_inputs(seed: int = 0) -> dict:
    key = jax.random.key(seed)
    ks = iter(jax.random.split(key, 64))
    nrm = lambda shape, s: jax.random.normal(next(ks), shape, jnp.float32) * s
    uni = lambda shape, lo, hi: jax.random.uniform(next(ks), shape, jnp.float32, lo, hi)
    D, H, N = D_MODEL, N_HEADS, HEAD_DIM
    s_in = D ** -0.5
    beta = DEEPNORM_BETA
    nv = N_A - 1
    return {
        'x': nrm((BATCH, SEQ, D), 1.0),
        'c': nrm((BATCH, D), 1.0),
        'ada_w': nrm((DEPTH, D, 6 * D), 0.1 * s_in),
        'ada_b': nrm((DEPTH, 6 * D), 0.01),
        'ln_g': 1.0 + nrm((DEPTH, 2, D), 0.02),
        'ln_b': nrm((DEPTH, 2, D), 0.02),
        'rw_mu': uni((N_A, 6, D), 0.0, 1.0),
        'rw_rkv': nrm((N_A, 3, D, D), s_in) * jnp.array([1.0, 1.0, beta], jnp.float32)[None, :, None, None],
        'rw_w0': uni((N_A, D), -6.0, -1.0),
        'rw_w1': nrm((N_A, D, DECAY_LORA), s_in),
        'rw_w2': nrm((N_A, DECAY_LORA, D), 0.1 * DECAY_LORA ** -0.5),
        'rw_a0': nrm((N_A, D), 0.1),
        'rw_a1': nrm((N_A, D, AAA_LORA), s_in),
        'rw_a2': nrm((N_A, AAA_LORA, D), 0.1 * AAA_LORA ** -0.5),
        'rw_g1': nrm((N_A, D, GATE_LORA), s_in),
        'rw_g2': nrm((N_A, GATE_LORA, D), GATE_LORA ** -0.5),
        'rw_kk': 0.85 + nrm((N_A, D), 0.02),
        'rw_ka': 1.0 + nrm((N_A, D), 0.02),
        'rw_rk': nrm((N_A, H, N), 0.1),
        'rw_gn_g': 1.0 + nrm((N_A, D), 0.02),
        'rw_gn_b': nrm((N_A, D), 0.02),
        'rw_wo': nrm((N_A, D, D), s_in * beta),
        'rw_v0': 1.0 + nrm((nv, D), 0.1),
        'rw_v1': nrm((nv, D, MV_LORA), s_in),
        'rw_v2': nrm((nv, MV_LORA, D), 0.1 * MV_LORA ** -0.5),
        'kv_ada_w': nrm((D, 2 * D), 0.1 * s_in),
        'kv_ada_b': nrm((2 * D,), 0.01),
        'kv_w': jnp.concatenate([nrm((D, D), s_in), nrm((D, D), s_in * beta), nrm((D, H), s_in)], axis=1),
        'kv_fb': uni((H,), 0.0, 5.0),
        'kv_knorm': 1.0 + nrm((N,), 0.02),
        'fx_wqg': nrm((N_B, D, 2 * D), s_in),
        'fx_qnorm': 1.0 + nrm((N_B, N), 0.02),
        'fx_wo': nrm((N_B, D, D), s_in * beta),
        'moe_wgrp': nrm((DEPTH, D, N_GROUPS), s_in),
        'moe_bgrp': nrm((DEPTH, N_GROUPS), 0.01),
        'moe_wexp': nrm((DEPTH, D, N_EXPERTS), s_in),
        'moe_bexp': nrm((DEPTH, N_EXPERTS), 0.01),
        'moe_wgate': nrm((DEPTH, N_EXPERTS, D, D_EXPERT), s_in),
        'moe_wup': nrm((DEPTH, N_EXPERTS, D, D_EXPERT), s_in),
        'moe_wdown': nrm((DEPTH, N_EXPERTS, D_EXPERT, D), D_EXPERT ** -0.5 * beta),
    }

def first_block(x, c, ada_w, ada_b, ln_g, ln_b, rw_mu, rw_rkv, rw_w0, rw_w1, rw_w2, rw_a0, rw_a1, rw_a2,
              rw_g1, rw_g2, rw_kk, rw_ka, rw_rk, rw_gn_g, rw_gn_b, rw_wo, rw_v0, rw_v1, rw_v2,
              kv_ada_w, kv_ada_b, kv_w, kv_fb, kv_knorm, fx_wqg, fx_qnorm, fx_wo,
              moe_wgrp, moe_bgrp, moe_wexp, moe_bexp, moe_wgate, moe_wup, moe_wdown):
    cs = jax.nn.silu(c)
    kv = None
    v_first = None
    for l in range(DEPTH):
        mod = cs @ ada_w[l] + ada_b[l]
        sh_m, sc_m, gt_m, sh_f, sc_f, gt_f = [m[:, None, :] for m in jnp.split(mod, 6, axis=-1)]
        h = x * (1 + sc_m) + sh_m
        if l < N_A:
            v_mix = None if l == 0 else (rw_v0[l - 1], rw_v1[l - 1], rw_v2[l - 1])
            y, v_first = rwkv7_time_mix(h, v_first, rw_mu[l], rw_rkv[l], rw_w0[l], rw_w1[l], rw_w2[l],
                                        rw_a0[l], rw_a1[l], rw_a2[l], rw_g1[l], rw_g2[l], rw_kk[l],
                                        rw_ka[l], rw_rk[l], rw_gn_g[l], rw_gn_b[l], rw_wo[l], v_mix)
        else:
            j = l - N_A
            y = fox_layer(h, kv, fx_wqg[j], fx_qnorm[j], fx_wo[j])
        x = layer_norm(DEEPNORM_ALPHA * x + (1 + gt_m) * y, ln_g[l, 0], ln_b[l, 0])
        h = x * (1 + sc_f) + sh_f
        y = hier_moe(h, moe_wgrp[l], moe_bgrp[l], moe_wexp[l], moe_bexp[l],
                     moe_wgate[l], moe_wup[l], moe_wdown[l])
        x = layer_norm(DEEPNORM_ALPHA * x + (1 + gt_f) * y, ln_g[l, 1], ln_b[l, 1])
        if l == N_A - 1:
            kv = shared_kv(x, cs, kv_ada_w, kv_ada_b, kv_w, kv_fb, kv_knorm)
    return x


DEPTH_2 = 1

GRID_W = 64
CTX_LEN = 256

F_GROUP_W = 128
F_WIDTH = D_MODEL // 2
F_GROUPS = F_WIDTH // F_GROUP_W

D_INNER = (3 * D_MODEL) // 2
SSD_HEAD_DIM = 64
SSD_HEADS = D_INNER // SSD_HEAD_DIM
SSD_GROUPS = 4
D_STATE = 128
CONV_W = 3
CHUNK = 128
CONV_CH = D_INNER + 2 * SSD_GROUPS * D_STATE

N_BRANCH = 2
P_IN = F_WIDTH + D_INNER + CONV_CH + 2 * SSD_HEADS + N_BRANCH * D_MODEL

N_EXPERTS_2 = 16
EC_FACTOR = 2
EXPERT_FF = D_MODEL

N_MOD = 6
RMS_EPS = 1e-6


def rms_norm(x, w):
    xf = x.astype(jnp.float32)
    y = xf * lax.rsqrt(jnp.mean(xf * xf, axis=-1, keepdims=True) + RMS_EPS)
    return (y * w.astype(jnp.float32)).astype(x.dtype)

def modulate(x, gain, shift, scale):
    return rms_norm(x, gain) * (1 + scale) + shift

def centred_dwconv(u, w, b, n_rows):
    bn, length, ch = u.shape
    row_len = length // n_rows
    r = u.reshape(bn, n_rows, row_len, ch)
    pad = CONV_W // 2
    rp = jnp.pad(r, ((0, 0), (0, 0), (pad, pad), (0, 0)))
    out = sum(rp[:, :, k:k + row_len] * w[k] for k in range(CONV_W)) + b
    return out.reshape(bn, length, ch)

def ssd_chunked(xh, dt, a, bm, cm, h0):
    bn, length, nh, hp = xh.shape
    g, n = bm.shape[2], bm.shape[3]
    hg = nh // g
    nc = length // CHUNK
    x = xh.reshape(bn, nc, CHUNK, g, hg, hp)
    dtc = dt.reshape(bn, nc, CHUNK, g, hg)
    bc = bm.reshape(bn, nc, CHUNK, g, n)
    cc = cm.reshape(bn, nc, CHUNK, g, n)
    acum = jnp.cumsum(dtc * a.reshape(g, hg), axis=2)
    xdt = x * dtc[..., None]
    seg = acum[:, :, :, None] - acum[:, :, None, :]
    lower = jnp.tril(jnp.ones((CHUNK, CHUNK), dtype=bool))[:, :, None, None]
    decay = jnp.where(lower, jnp.exp(jnp.where(lower, seg, 0.0)), 0.0)
    cb = jnp.einsum('bctgn,bcsgn->bctsg', cc, bc)
    y_diag = jnp.einsum('bctsg,bctsgh,bcsghp->bctghp', cb, decay, xdt)
    decay_end = jnp.exp(acum[:, :, -1:] - acum)
    states = jnp.einsum('bcsgn,bcsgh,bcsghp->bcghpn', bc, decay_end, xdt)
    chunk_decay = jnp.exp(acum[:, :, -1])

    def step(h, inp):
        dec, st = inp
        return dec[..., None, None] * h + st, h

    h_final, h_prev = lax.scan(step, h0, (jnp.moveaxis(chunk_decay, 1, 0), jnp.moveaxis(states, 1, 0)))
    h_prev = jnp.moveaxis(h_prev, 0, 1)
    y_off = jnp.einsum('bctgn,bctgh,bcghpn->bctghp', cc, jnp.exp(acum), h_prev)
    y = (y_diag + y_off).reshape(bn, length, nh, hp)
    return y, h_final

def bidir_ssd(xh, dt_raw, bm, cm, dt_bias, a_log, h0_f, h0_b):
    dt_f = jax.nn.softplus(dt_raw[:, :, 0] + dt_bias[0])
    dt_b = jax.nn.softplus(dt_raw[:, :, 1] + dt_bias[1])
    a_f = -jnp.exp(a_log[0].astype(jnp.float32))
    a_b = -jnp.exp(a_log[1].astype(jnp.float32))
    y_f, h_f = ssd_chunked(xh, dt_f, a_f, bm, cm, h0_f)
    flip = lambda t: jnp.flip(t, axis=1)
    y_b, h_b = ssd_chunked(flip(xh), flip(dt_b), a_b, flip(bm), flip(cm), h0_b)
    return y_f + flip(y_b), h_f, h_b

def token_mixer(h, n_rows, h0_f, h0_b, w_in, conv_w, conv_b, dt_bias, a_log, d_skip, ssd_norm,
                w_fourier, w_ssd_out, b_gate, w_out):
    bn, length, _ = h.shape
    proj = h @ w_in
    i1 = F_WIDTH
    i2 = i1 + D_INNER
    i3 = i2 + CONV_CH
    i4 = i3 + 2 * SSD_HEADS
    u_f, z, xbc, dt_raw, gate_logits = jnp.split(proj, [i1, i2, i3, i4], axis=-1)
    uf = u_f.reshape(bn, length, F_GROUPS, F_GROUP_W).astype(jnp.float32)
    f = jnp.fft.fft2(uf, axes=(1, 3), norm='ortho').real.astype(h.dtype).reshape(bn, length, F_WIDTH)
    f_branch = f @ w_fourier
    xbc = jax.nn.silu(centred_dwconv(xbc, conv_w, conv_b, n_rows))
    xs, bm, cm = jnp.split(xbc, [D_INNER, D_INNER + SSD_GROUPS * D_STATE], axis=-1)
    xh = xs.reshape(bn, length, SSD_HEADS, SSD_HEAD_DIM).astype(jnp.float32)
    bm = bm.reshape(bn, length, SSD_GROUPS, D_STATE).astype(jnp.float32)
    cm = cm.reshape(bn, length, SSD_GROUPS, D_STATE).astype(jnp.float32)
    dt_raw = dt_raw.reshape(bn, length, 2, SSD_HEADS).astype(jnp.float32)
    y, h_f, h_b = bidir_ssd(xh, dt_raw, bm, cm, dt_bias, a_log, h0_f, h0_b)
    y = y + d_skip[:, None].astype(jnp.float32) * xh
    y = y.reshape(bn, length, D_INNER).astype(h.dtype)
    y = rms_norm(y * jax.nn.silu(z), ssd_norm)
    s_branch = y @ w_ssd_out
    g = jax.nn.sigmoid(gate_logits.reshape(bn, length, N_BRANCH, D_MODEL) + b_gate)
    merged = g[:, :, 0] * f_branch + g[:, :, 1] * s_branch
    return merged @ w_out, h_f, h_b

def expert_choice_ffn(h, w_router, w_e_gate, w_e_up, w_e_down):
    bn, length, d = h.shape
    cap = EC_FACTOR * length // N_EXPERTS_2
    aff = jax.nn.softmax((h @ w_router).astype(jnp.float32), axis=-1)
    top_aff, top_idx = lax.top_k(jnp.swapaxes(aff, 1, 2), cap)
    xe = jax.vmap(lambda hb, ib: hb[ib])(h, top_idx)
    hid = jax.nn.silu(jnp.einsum('becd,edf->becf', xe, w_e_gate)) * jnp.einsum('becd,edf->becf', xe, w_e_up)
    ye = jnp.einsum('becf,efd->becd', hid, w_e_down) * top_aff[..., None].astype(h.dtype)
    return jax.vmap(lambda ib, yb: jnp.zeros((length, d), yb.dtype).at[ib.reshape(-1)].add(yb.reshape(-1, d)))(top_idx, ye)

def second_inputs(seed: int = 0) -> dict:
    key = jax.random.key(seed)
    ks = jax.random.split(key, 32)
    nrm = lambda k, shape, s: jax.random.normal(k, shape, jnp.float32) * s
    L = DEPTH_2
    dt0 = jnp.exp(jax.random.uniform(ks[12], (L, 2, SSD_HEADS), jnp.float32, np.log(1e-3), np.log(1e-1)))
    return {
        'x': nrm(ks[0], (BATCH, SEQ, D_MODEL), 1.0),
        'c': nrm(ks[1], (BATCH, D_MODEL), 1.0),
        'ctx': nrm(ks[2], (BATCH, CTX_LEN, D_MODEL), 1.0),
        'c_ctx': nrm(ks[3], (D_MODEL,), 1.0),
        'w_mod': nrm(ks[4], (L, D_MODEL, N_MOD * D_MODEL), 0.5 * D_MODEL ** -0.5),
        'b_mod': nrm(ks[5], (L, N_MOD * D_MODEL), 0.02),
        'norm_mix_pre': 1.0 + nrm(ks[6], (L, D_MODEL), 0.05),
        'norm_mix_post': 1.0 + nrm(ks[7], (L, D_MODEL), 0.05),
        'norm_ffn_pre': 1.0 + nrm(ks[8], (L, D_MODEL), 0.05),
        'norm_ffn_post': 1.0 + nrm(ks[9], (L, D_MODEL), 0.05),
        'w_in': nrm(ks[10], (L, D_MODEL, P_IN), D_MODEL ** -0.5),
        'conv_w': nrm(ks[11], (L, CONV_W, CONV_CH), CONV_W ** -0.5),
        'conv_b': nrm(ks[13], (L, CONV_CH), 0.02),
        'dt_bias': dt0 + jnp.log(-jnp.expm1(-dt0)),
        'a_log': jnp.log(jax.random.uniform(ks[14], (L, 2, SSD_HEADS), jnp.float32, 1.0, 16.0)),
        'd_skip': 1.0 + nrm(ks[15], (L, SSD_HEADS), 0.1),
        'ssd_norm': 1.0 + nrm(ks[16], (L, D_INNER), 0.05),
        'w_fourier': nrm(ks[17], (L, F_WIDTH, D_MODEL), F_WIDTH ** -0.5),
        'w_ssd_out': nrm(ks[18], (L, D_INNER, D_MODEL), D_INNER ** -0.5),
        'b_gate': nrm(ks[19], (L, N_BRANCH, D_MODEL), 0.1),
        'w_out': nrm(ks[20], (L, D_MODEL, D_MODEL), D_MODEL ** -0.5),
        'w_router': nrm(ks[21], (L, D_MODEL, N_EXPERTS_2), D_MODEL ** -0.5),
        'w_e_gate': nrm(ks[22], (L, N_EXPERTS_2, D_MODEL, EXPERT_FF), D_MODEL ** -0.5),
        'w_e_up': nrm(ks[23], (L, N_EXPERTS_2, D_MODEL, EXPERT_FF), D_MODEL ** -0.5),
        'w_e_down': nrm(ks[24], (L, N_EXPERTS_2, EXPERT_FF, D_MODEL), EXPERT_FF ** -0.5),
    }

def second_block(x, c, ctx, c_ctx, w_mod, b_mod, norm_mix_pre, norm_mix_post, norm_ffn_pre, norm_ffn_post,
              w_in, conv_w, conv_b, dt_bias, a_log, d_skip, ssd_norm, w_fourier, w_ssd_out, b_gate, w_out,
              w_router, w_e_gate, w_e_up, w_e_down):
    bn, length, d = x.shape
    rows = length // GRID_W
    hx, hc = x, ctx
    for l in range(DEPTH_2):
        mod_x = (jax.nn.silu(c) @ w_mod[l] + b_mod[l]).reshape(bn, N_MOD, 1, d)
        mod_c = (jax.nn.silu(c_ctx) @ w_mod[l] + b_mod[l]).reshape(N_MOD, d)
        sh1, sc1, g1, sh2, sc2, g2 = [mod_x[:, i] for i in range(N_MOD)]
        csh1, csc1, cg1, csh2, csc2, cg2 = [mod_c[i] for i in range(N_MOD)]
        mix_w = (w_in[l], conv_w[l], conv_b[l], dt_bias[l], a_log[l], d_skip[l], ssd_norm[l],
                 w_fourier[l], w_ssd_out[l], b_gate[l], w_out[l])
        h0 = jnp.zeros((bn, SSD_GROUPS, SSD_HEADS // SSD_GROUPS, SSD_HEAD_DIM, D_STATE), jnp.float32)
        mix_c, hf_c, hb_c = token_mixer(modulate(hc, norm_mix_pre[l], csh1, csc1), 1, h0, h0, *mix_w)
        mix_x, _, _ = token_mixer(modulate(hx, norm_mix_pre[l], sh1, sc1), rows, hf_c, hb_c, *mix_w)
        hx = hx + g1 * rms_norm(mix_x, norm_mix_post[l])
        ffn_x = expert_choice_ffn(modulate(hx, norm_ffn_pre[l], sh2, sc2), w_router[l], w_e_gate[l], w_e_up[l], w_e_down[l])
        hx = hx + g2 * rms_norm(ffn_x, norm_ffn_post[l])
        if l + 1 < DEPTH_2:
            hc = hc + cg1 * rms_norm(mix_c, norm_mix_post[l])
            ffn_c = expert_choice_ffn(modulate(hc, norm_ffn_pre[l], csh2, csc2), w_router[l], w_e_gate[l], w_e_up[l], w_e_down[l])
            hc = hc + cg2 * rms_norm(ffn_c, norm_ffn_post[l])
    return hx


def setup_inputs(seed=0):
    out = dict(first_inputs(seed))
    for name, value in second_inputs(seed + 1).items():
        if name != "x":
            out[name + "_2"] = value
    return out


def reference(
    x, c, ada_w, ada_b, ln_g, ln_b, rw_mu, rw_rkv, rw_w0, rw_w1, rw_w2, rw_a0, rw_a1, rw_a2,
    rw_g1, rw_g2, rw_kk, rw_ka, rw_rk, rw_gn_g, rw_gn_b, rw_wo, rw_v0, rw_v1, rw_v2, kv_ada_w,
    kv_ada_b, kv_w, kv_fb, kv_knorm, fx_wqg, fx_qnorm, fx_wo, moe_wgrp, moe_bgrp, moe_wexp,
    moe_bexp, moe_wgate, moe_wup, moe_wdown, c_2, ctx_2, c_ctx_2, w_mod_2, b_mod_2,
    norm_mix_pre_2, norm_mix_post_2, norm_ffn_pre_2, norm_ffn_post_2, w_in_2, conv_w_2,
    conv_b_2, dt_bias_2, a_log_2, d_skip_2, ssd_norm_2, w_fourier_2, w_ssd_out_2, b_gate_2,
    w_out_2, w_router_2, w_e_gate_2, w_e_up_2, w_e_down_2,
):
    x = first_block(
        x, c, ada_w, ada_b, ln_g, ln_b, rw_mu, rw_rkv, rw_w0, rw_w1, rw_w2, rw_a0, rw_a1, rw_a2,
        rw_g1, rw_g2, rw_kk, rw_ka, rw_rk, rw_gn_g, rw_gn_b, rw_wo, rw_v0, rw_v1, rw_v2,
        kv_ada_w, kv_ada_b, kv_w, kv_fb, kv_knorm, fx_wqg, fx_qnorm, fx_wo, moe_wgrp, moe_bgrp,
        moe_wexp, moe_bexp, moe_wgate, moe_wup, moe_wdown,
    )
    return second_block(
        x, c_2, ctx_2, c_ctx_2, w_mod_2, b_mod_2, norm_mix_pre_2, norm_mix_post_2,
        norm_ffn_pre_2, norm_ffn_post_2, w_in_2, conv_w_2, conv_b_2, dt_bias_2, a_log_2,
        d_skip_2, ssd_norm_2, w_fourier_2, w_ssd_out_2, b_gate_2, w_out_2, w_router_2,
        w_e_gate_2, w_e_up_2, w_e_down_2,
    )


_drawn_inputs = setup_inputs


def setup_inputs(seed=0):
    import zlib

    import numpy as np

    out = dict(_drawn_inputs(seed))
    spreads = {}
    factors = {'rw_w1': 3.987,
     'rw_w2': 5.502,
     'rw_kk': 3.457,
     'rw_ka': 3.32,
     'rw_gn_b': 3.173,
     'kv_ada_b': 4.297,
     'kv_knorm': 8.0,
     'fx_qnorm': 8.0,
     'moe_bgrp': 3.036,
     'moe_bexp': 3.516,
     'norm_ffn_post_2': 4.014,
     'conv_b_2': 3.649}
    for name, (base, spread) in spreads.items():
        noise = np.random.default_rng([zlib.crc32(name.encode()), seed]).standard_normal(out[name].shape)
        drawn = base * np.exp(spread * noise) if base else spread * noise
        out[name] = __import__('jax').numpy.asarray(drawn.astype(out[name].dtype))
    for name, factor in factors.items():
        out[name] = (out[name] * factor).astype(out[name].dtype)
    return out
```

```python
import math
from contextlib import ExitStack

import concourse.bass as bass
from concourse import mybir

F32 = mybir.dt.float32
ALU = mybir.AluOpType
ACT = mybir.ActivationFunctionType
AX = mybir.AxisListType

P = 128
T = 512
D = 1024
KT = D // P
TT = T // P
HEADS, HD = 16, 64
CTX = 256
SLOT = KT * T
DEPTH = 2
ALPHA = (2 * DEPTH) ** 0.25
NG, EPG = 4, 8
NE = NG * EPG
DE = 512
SEATS = 64
CH = 32
NC = T // CH
DI, SSD_H, SSD_G, NS = 1536, 24, 4, 128
DIT = DI // P
XBC = DI + 2 * SSD_G * NS
XT = XBC // P
FW = 512
FT = FW // P
NE2, FF2 = 16, 1024
CAP = 2 * T // NE2
ROW = 64


class Own:

    def __init__(self, eng, sem, i=None, per=0):
        self.eng, self.sem, self.n, self.i, self.per = eng, sem, 0, i, per

    def mark(self, ins):
        ins.then_inc(self.sem, 1)
        self.n += 1

    def join(self):
        self.eng.wait_ge(self.sem, self.n if self.i is None else self.i * self.per + self.n)

    def seal(self, ins):
        ins.then_inc(self.sem, 1)
        self.n += 1
        self.eng.wait_ge(self.sem, self.n if self.i is None else self.i * self.per + self.n)


class Steps:

    def __init__(self, sem, names, lead=0):
        self.sem, self.names, self.base = sem, names, 1 + lead * len(names)

    def at(self, name, i=0):
        return i * len(self.names) + (self.names.index(name) + 1 + self.base)

    def before(self, i=0):
        return i * len(self.names) + self.base


class Stage:

    number, used = 0, []

    def __init__(self, nc):
        self.nc, self.ctx = nc, ExitStack()

    def __enter__(self):
        self.own = []
        Stage.number += 1
        return self

    def sem(self, name):
        self.own.append(self.nc.alloc_semaphore(name=f"{name}_{Stage.number}"))
        return self.own[-1]

    def sems(self, name, n):
        return [self.sem(f"{name}{j}") for j in range(n)]

    def block(self):
        if Stage.used:
            self.nc.clear_and_free_semaphores(Stage.used)
        Stage.used = self.own
        return self.ctx.enter_context(self.nc.Block())

    def __exit__(self, *e):
        return self.ctx.__exit__(*e)


def loop(eng, n, body):
    if n == 1:
        body(0)
    elif n > 1:
        with eng.Fori(0, n) as i:
            body(i)


def bc(ap, shape):
    return ap.broadcast_to(shape)


class Core:

    def __init__(self, nc, ctx, ins, cols):
        self.nc, self.ins, self.cols = nc, ins, cols
        sb = lambda n, s: ctx.enter_context(nc.sbuf_tensor(n, s, F32))
        self.arena = sb("arena", [P, 12, SLOT])
        self.vec = sb("vec", [P, ins["vecs"].shape[1]])
        self.ones = sb("ones", [P, P])
        self.mean = sb("mean", [P, P])
        self.small = sb("small", [P, 2560])
        self.ident = sb("ident", [P, P])
        self.blk = sb("blk", [P, P])
        self.mod = [sb(f"mod{l}", [P, 48]) for l in range(DEPTH)]
        self.modkv = sb("modkv", [P, 16])
        self.mod2 = sb("mod2", [P, 48, 2])
        n = TT * (NE + 2)
        self.places, self.gates = (self.small[:, 1960 + j * n:1960 + (j + 1) * n].rearrange("p (t e) -> p t e", t=TT) for j in range(2))
        self.crowded = self.small[0:1, 2300:2301].bitcast(mybir.dt.int32)
        self.cs = sb("cs", [P, KT, 3])
        self.ps = ctx.enter_context(nc.psum_tensor("ps", [P, 8, 512], F32))

    def slot(self, n, tok=T):
        return self.arena[:, n, 0:KT * tok].rearrange("p (k t) -> p k t", t=tok)

    def tiles(self, n, k, tok=T):
        flat = self.arena[:, :, :].rearrange("p a b -> p (a b)")
        return flat[:, n * SLOT:n * SLOT + k * tok].rearrange("p (k t) -> p k t", t=tok)

    def at(self, tile, k, tok=T):
        flat = self.arena[:, :, :].rearrange("p a b -> p (a b)")
        return flat[:, tile * T:tile * T + k * tok].rearrange("p (k t) -> p k t", t=tok)

    def flat(self, tile, n):
        return self.arena[:, :, :].rearrange("p a b -> p (a b)")[:, tile * T:tile * T + n]

    def v(self, name, k=0):
        a = self.cols[name][0] + k
        return self.vec[:, a:a + 1]

    def vs(self, name):
        a, n = self.cols[name]
        return self.vec[:, a:a + n]

    def row(self, name):
        return self.ins[name]


def setup(K):
    nc = K.nc
    with Stage(nc) as S:
        loaded, own_d, own_a = S.sem("loaded"), S.sem("own_d"), S.sem("own_a")
        block = S.block()

        @block.sync
        def _(sp):
            sp.dma_start(K.vec[:, :], K.ins["vecs"]).then_inc(loaded, 16)
            sp.dma_start(K.ident[:, :], K.ins["c_ident"]).then_inc(loaded, 16)
            sp.dma_start(K.blk[:, :], K.ins["c_blk"]).then_inc(loaded, 16)
            sp.dma_start(K.slot(0), K.ins["xT"].rearrange("(k p) t -> p k t", p=P)).then_inc(loaded, 16)

        @block.vector
        def _(dve):
            o = Own(dve, own_d)
            o.seal(nc.vector.memset(K.ones[:, :], 1.0))
            o.seal(nc.vector.memset(K.mean[:, :], 1.0 / D))
            dve.wait_ge(loaded, 64)
            o.seal(nc.vector.tensor_scalar(K.vs("qnorm8"), K.vs("qnorm"), HD ** -0.5, None, ALU.mult))

        @block.scalar
        def _(act):
            act.wait_ge(loaded, 64)
            o = Own(act, own_a)
            for n, name in enumerate(("c", "c_2", "c_ctx_2")):
                o.seal(nc.scalar.activation(K.cs[:, :, n], K.vs(name), ACT.Silu))


def modulation(K, W, ncols, first, nv, bias, dst, ones_at):
    nc = K.nc
    W = W.rearrange("(k p) n -> p k n", p=P)
    B = 4
    wb = [K.slot(n) for n in (6, 7, 9, 10)]
    KD = KT if nv == 1 else 6
    part = K.slot(8)
    n = ncols // 512
    sums = K.ps[:, 0, 0:4 * n * nv]
    with Stage(nc) as S:
        w_in, rounds, own = S.sems("w_in", B), S.sem("pe_rounds"), S.sem("own")
        pe_s = Steps(S.sem("pe_steps"), [f"chunk{b}" for b in range(B)], lead=1)
        dve_s = Steps(S.sem("dve_steps"), [f"b{b}k{k}v{v}" for b in range(B) for k in range(KD) for v in range(nv)], lead=1)
        block = S.block()

        @block.sync
        def _(sp):
            def body(i):
                for b in range(B):
                    sp.wait_ge(pe_s.sem, pe_s.at(f"chunk{b}", i - 1))
                    sp.dma_start(wb[b], W[:, :, bass.ds(i * (B * 512) + b * 512, 512)]).then_inc(w_in[b], 16)
            loop(sp, n // B, body)

        @block.tensor
        def _(pe):
            pe.sem_inc(pe_s.sem, pe_s.base)

            def body(i):
                for b in range(B):
                    pe.wait_ge(w_in[b], i * 16 + 16)
                    pe.wait_ge(dve_s.sem, dve_s.at(f"b{b}k{KD - 1}v{nv - 1}", i))
                    pe.sem_inc(rounds, 1)
                    for m in range(4):
                        at = i * (4 * B * nv) + (b * 4 + m) * nv
                        tile = slice(m * P, (m + 1) * P)
                        for k in range(KD, KT):
                            nc.tensor.matmul(sums[:, bass.ds(at, nv)], wb[b][:, k, tile], K.cs[:, k, first:first + nv],
                                             start=(k == KD), stop=False, skip_group_check=True)
                        for v in range(nv):
                            mm = nc.tensor.matmul(sums[:, bass.ds(at + v, 1)], part[:, 2 * b + v, tile], K.ones[:, 0:1],
                                                  start=(KD == KT), stop=True, skip_group_check=True)
                    mm.then_inc(pe_s.sem, 1)
            loop(pe, n // B, body)

        @block.vector
        def _(dve):
            dve.sem_inc(dve_s.sem, dve_s.base)

            def body(i):
                for b in range(B):
                    dve.wait_ge(w_in[b], i * 16 + 16)
                    dve.wait_ge(pe_s.sem, pe_s.at(f"chunk{b}", i - 1))
                    for k in range(KD):
                        for v in range(nv):
                            c, to = K.cs[:, k, first + v:first + v + 1], part[:, 2 * b + v, :]
                            if k == 0:
                                ins = nc.vector.tensor_scalar(to, wb[b][:, k, :], c, None, ALU.mult)
                            else:
                                dve.wait_ge(dve_s.sem, dve_s.at(f"b{b}k{k - 1}v{v}", i))
                                ins = nc.vector.scalar_tensor_tensor(out=to, in0=wb[b][:, k, :], scalar=c, in1=to, op0=ALU.mult, op1=ALU.add)
                            ins.then_inc(dve_s.sem, 1)
            loop(dve, n // B, body)
            o = Own(dve, own)
            dve.wait_ge(pe_s.sem, pe_s.before(n // B))
            if nv == 1:
                o.seal(nc.vector.tensor_tensor(dst[:, :], sums, bias, ALU.add))
            else:
                o.seal(nc.vector.tensor_tensor(dst[:, :, :], sums.rearrange("p (m v) -> p m v", v=nv), bc(bias.unsqueeze(2), [P, 4 * n, nv]), ALU.add))
            for a in ones_at:
                d = dst[:, a:a + KT] if nv == 1 else dst[:, a:a + KT, :]
                o.seal(nc.vector.tensor_scalar(d, d, 1.0, None, ALU.add))


def linear(K, W, ncols, rhs, evac, wslot=9, kt=KT, tok=T, pre=None, n_pre=0):
    nc = K.nc
    W = W.rearrange("(k p) n -> p k n", p=P)
    wb = [K.tiles(wslot, 2 * kt, 512)[:, b * kt:(b + 1) * kt, :] for b in range(2)]
    n = ncols // 512
    with Stage(nc) as S:
        w_in, ready, free = [S.sems(f"w{b}_in", 2) for b in range(2)], S.sem("tile_ready"), S.sem("tile_free")
        made = S.sem("rhs_made")
        block = S.block()

        def chunks(eng, one):
            loop(eng, n // 2, lambda i: [one(i, b) for b in range(2)])
            if n % 2:
                one(n // 2, 0)

        @block.sync
        def _(sp):
            def one(i, b):
                sp.wait_ge(free, i * 8 + b * 4 + 4)
                for j in range(2):
                    sp.dma_start(wb[b][:, :, j * 256:(j + 1) * 256],
                                 W[:, :, bass.ds(i * 1024 + (b * 512 + j * 256), 256)]).then_inc(w_in[b][j], 16)
            chunks(sp, one)

        @block.tensor
        def _(pe):
            if pre:
                pe.wait_ge(made, n_pre)

            def one(i, b):
                for m in range(4):
                    if m % 2 == 0:
                        pe.wait_ge(w_in[b][m // 2], i * 16 + 16)
                    pe.wait_ge(free, i * 8 + b * 4 + m + 1)
                    for k in range(kt):
                        mm = nc.tensor.matmul(K.ps[:, b * 4 + m, 0:tok], wb[b][:, k, m * P:(m + 1) * P], rhs[:, k, :],
                                              start=(k == 0), stop=(k == kt - 1))
                    mm.then_inc(ready, 1)
            chunks(pe, one)

        if pre:
            @block.vector
            def _(dve):
                pre(dve, made)

        @block.scalar
        def _(act):
            act.sem_inc(free, 8)

            def one(i, b):
                for m in range(4):
                    act.wait_ge(ready, i * 8 + b * 4 + m + 1)
                    evac(act, K.ps[:, b * 4 + m, 0:tok], i * 8 + b * 4 + m).then_inc(free, 1)
            chunks(act, one)


def to_slot(nc, dst, func=None, bias=None):
    def evac(act, ps, tile):
        kw = {"bias": bias[:, bass.ds(tile, 1)]} if bias is not None else {}
        return nc.scalar.activation(dst[:, bass.ds(tile, 1), :], ps.unsqueeze(1), func or ACT.Copy, **kw)
    return evac


def vector_stage(K, work):
    with Stage(K.nc) as S:
        own = S.sem("own")
        block = S.block()

        @block.vector
        def _(dve):
            work(dve, Own(dve, own))


def scale_shift(K, src, dst, scale, shift, kt=KT):
    nc = K.nc
    with Stage(nc) as S:
        by_dve, by_act = S.sem("by_dve"), S.sem("by_act")
        block = S.block()

        @block.vector
        def _(dve):
            for k in range(0, kt, 2):
                nc.vector.tensor_scalar(dst[:, k, :], src[:, k, :], scale(k), shift(k), ALU.mult, ALU.add).then_inc(by_dve, 1)

        @block.scalar
        def _(act):
            for k in range(1, kt, 2):
                nc.scalar.activation(dst[:, k, :], src[:, k, :], ACT.Identity, scale=scale(k), bias=shift(k)).then_inc(by_act, 1)


def normalise(K, z, dst, tmp, ones, inv, eps, centre, gain, shift, kt=KT, tok=T, per_tile=False,
              keep=None):
    nc = K.nc
    groups = [[k] for k in range(kt)] if per_tile else [list(range(kt))]
    group_of = lambda k: k if per_tile else 0
    n = len(groups)
    assert n <= 8
    rs = tmp[0:HEADS if per_tile else P, 0, :]
    first = 1 if centre and not per_tile else 0
    w = z if keep is None else keep
    pick, spread = K.small[:, 900:930], K.small[0:HEADS, 932:932 + D]
    with Stage(nc) as S:
        loaded, spread_out = S.sem("loaded"), S.sem("spread")
        mean, cent, sq, var, root, recip, normed, moved = (S.sem(x) for x in (
            "mean", "centred", "squared", "var", "root", "reciprocal", "normed", "moved"))
        block = S.block()

        @block.tensor
        def _(pe):
            if centre:
                for g, ks in enumerate(groups):
                    for k in ks:
                        mm = nc.tensor.matmul(K.ps[:, g, 0:tok], ones, z[:, k, :], start=(k == ks[0]), stop=(k == ks[-1]))
                    mm.then_inc(mean, 1)
            if per_tile:
                pe.wait_ge(loaded, 32)
            for k in range(kt):
                pe.wait_ge(sq, k + 1)
                to, lhs = (K.ps[0:HEADS, 0, 0:tok], pick[:, 14 - 2 * k:30 - 2 * k]) if per_tile else (K.ps[:, first, 0:tok], ones)
                mm = nc.tensor.matmul(to, lhs, tmp[:, k, :], start=(k == 0), stop=(k == kt - 1))
            mm.then_inc(var, 1)
            if per_tile:
                pe.wait_ge(recip, 1)
                for k in range(kt):
                    nc.tensor.matmul(K.ps[:, k, 0:tok], spread[:, k * P:(k + 1) * P], tmp[0:HEADS, 0, :],
                                     start=True, stop=True).then_inc(spread_out, 1)

        if per_tile:
            @block.sync
            def _(sp):
                sp.dma_start(pick, K.ins["c_pick"]).then_inc(loaded, 16)
                sp.dma_start(spread, K.ins["c_spread"]).then_inc(loaded, 16)

        @block.vector
        def _(dve):
            if centre:
                for k in range(kt):
                    dve.wait_ge(mean, group_of(k) + 1)
                    nc.vector.scalar_tensor_tensor(out=z[:, k, :], in0=K.ps[:, group_of(k), 0:tok], scalar=-inv if per_tile else -1.0,
                                                   in1=z[:, k, :], op0=ALU.mult, op1=ALU.add).then_inc(cent, 1)
            dve.wait_ge(root, 1)
            nc.vector.reciprocal(rs, rs).then_inc(recip, 1)
            dve.wait_ge(recip, 1)
            if centre:
                dve.wait_ge(cent, kt)
            for k in range(kt):
                if per_tile:
                    dve.wait_ge(spread_out, k + 1)
                nc.vector.tensor_tensor(w[:, k, :], z[:, k, :], K.ps[:, k, 0:tok] if per_tile else rs, ALU.mult).then_inc(normed, 1)

        @block.scalar
        def _(act):
            for k in range(kt):
                if centre:
                    act.wait_ge(cent, k + 1)
                nc.scalar.activation(tmp[:, k, :], z[:, k, :], ACT.Square).then_inc(sq, 1)
            act.wait_ge(var, 1)
            rows = slice(0, HEADS if per_tile else P)
            nc.scalar.activation(rs, K.ps[rows, first, 0:tok], ACT.Sqrt, scale=inv, bias=eps[rows, :]).then_inc(root, 1)
            for k in range(kt):
                act.wait_ge(normed, k + 1)
                nc.scalar.activation(dst[:, k, :], w[:, k, :], ACT.Identity, scale=gain(k),
                                     bias=K.v("zero") if shift is None else shift(k)).then_inc(moved, 1)



S_X, S_H, S_R, S_K, S_V, S_LW, S_A, S_G, S_Y, S_W0, S_W1, S_KK = range(12)


def mixed(K, n, dst, src=None):
    nc = K.nc
    h, xx = K.slot(S_H), K.slot(S_KK)

    def pre(dve, done):
        for k in range(KT):
            nc.vector.scalar_tensor_tensor(out=dst[:, k, :], in0=xx[:, k, :], scalar=K.v("mu", n * KT + k),
                                           in1=h[:, k, :], op0=ALU.mult, op1=ALU.add).then_inc(done, 1)
    return pre


def lora(K, n, w1, w2, rank, mid, out, bias, dst):
    nc = K.nc
    h = K.slot(S_Y)
    parts = [(a, min(P, rank - a)) for a in range(0, rank, P)]
    wa = K.tiles(S_W0, KT, rank)
    wb = K.tiles(S_W1, len(parts), D)
    mid_sb = K.tiles(S_W1, 4, T)[:, 2:4, :] if len(parts) == 1 else K.tiles(S_W1, 8, T)[:, 4:6, :]
    with Stage(nc) as S:
        w_in, made, down, midd, up, free = (S.sem(x) for x in ("w_in", "mix_made", "down_ready", "mid_made", "up_ready", "up_free"))
        block = S.block()

        @block.sync
        def _(sp):
            sp.dma_start(wa, w1.rearrange("(k p) n -> p k n", p=P)).then_inc(w_in, 16)
            for j, (a, r) in enumerate(parts):
                sp.dma_start(wb[0:r, j, :], w2[a:a + r, :]).then_inc(w_in, 16)

        @block.vector
        def _(dve):
            mixed(K, n, h)(dve, made)

        @block.tensor
        def _(pe):
            pe.wait_ge(w_in, 16 + 16 * len(parts))
            pe.wait_ge(made, KT)
            for j, (a, r) in enumerate(parts):
                for k in range(KT):
                    mm = nc.tensor.matmul(K.ps[0:r, j, :], wa[:, k, a:a + r], h[:, k, :], start=(k == 0), stop=(k == KT - 1))
                mm.then_inc(down, 1)
            pe.wait_ge(midd, len(parts))
            for m in range(KT):
                if m >= 6:
                    pe.wait_ge(free, m - 5)
                for j, (a, r) in enumerate(parts):
                    mm = nc.tensor.matmul(K.ps[:, 2 + m % 6, :], wb[0:r, j, m * P:(m + 1) * P], mid_sb[0:r, j, :],
                                          start=(j == 0), stop=(j == len(parts) - 1))
                mm.then_inc(up, 1)

        @block.scalar
        def _(act):
            for j, (a, r) in enumerate(parts):
                act.wait_ge(down, j + 1)
                nc.scalar.activation(mid_sb[0:r, j, :], K.ps[0:r, j, :], mid).then_inc(midd, 1)
            for m in range(KT):
                act.wait_ge(up, m + 1)
                kw = {"bias": K.v(bias, m)} if bias else {}
                nc.scalar.activation(dst[:, m, :], K.ps[:, 2 + m % 6, :], out, **kw).then_inc(free, 1)


def head_sums(K, src, n_out_banks=KT):
    for k in range(KT):
        mm = K.nc.tensor.matmul(K.ps[:, k, :], K.blk[:, :], src[:, k, :], start=True, stop=True)
    return mm


def wkv_inputs(K):
    nc = K.nc
    r, k, v, lw, a, y, w0, w1, kk = (K.slot(n) for n in (S_R, S_K, S_V, S_LW, S_A, S_Y, S_W0, S_W1, S_KK))
    with Stage(nc) as S:
        raw, sq, ss, root, kka, rk, rks, ex, own = (S.sem(x) for x in (
            "keys", "squared", "sums", "root", "keys_used", "rk_made", "rk_sums", "exps", "own"))
        block = S.block()
        reset = K.small[:, 0:T]
        gaps = K.small[:, 0:T].rearrange("p (c t) -> p c t", t=CH)

        @block.vector
        def _(dve):
            o = Own(dve, own)
            for t in range(KT):
                o.mark(nc.vector.tensor_scalar(kk[:, t, :], k[:, t, :], K.v("kk", t), None, ALU.mult))
            o.seal(nc.vector.memset(reset, 1.0))
            o.seal(nc.vector.memset(gaps[:, :, 0:1], 0.0))
            nc.vector.tensor_tensor(w0, kk, kk, ALU.mult).then_inc(sq, 1)
            o.seal(nc.vector.tensor_scalar(lw, lw, -math.exp(-0.5), None, ALU.mult))
            for t in range(KT):
                o.mark(nc.vector.tensor_tensor_scan(w1[:, t, :], reset, lw[:, t, :], 0.0, ALU.mult, ALU.add))
            o.join()
            nc.vector.tensor_tensor(lw, w1, lw, ALU.subtract).then_inc(raw, 1)
            dve.wait_ge(root, 1)
            o.seal(nc.vector.tensor_scalar(w0, w0, 1e-12, None, ALU.max))
            o.seal(nc.vector.reciprocal(w0, w0))
            o.seal(nc.vector.tensor_tensor(kk, kk, w0, ALU.mult))
            for t in range(KT):
                o.mark(nc.vector.tensor_scalar(w0[:, t, :], a[:, t, :], -1.0, K.v("ka", t), ALU.add, ALU.mult))
            o.join()
            o.seal(nc.vector.scalar_tensor_tensor(out=k, in0=w0, scalar=1.0, in1=k, op0=ALU.add, op1=ALU.mult))
            o.seal(nc.vector.tensor_tensor(w0, r, k, ALU.mult))
            for t in range(KT):
                nc.vector.tensor_scalar(w0[:, t, :], w0[:, t, :], K.v("rk", t), None, ALU.mult).then_inc(rk, 1)
            o.seal(nc.vector.tensor_tensor(a, a, kk, ALU.mult))
            dve.wait_ge(rks, 1)
            o.seal(nc.vector.tensor_tensor(w0, K.ps[:, :, :], v, ALU.mult))
            dve.wait_ge(ex, 1)
            o.seal(nc.vector.scalar_tensor_tensor(out=kk, in0=kk, scalar=-1.0, in1=y, op0=ALU.mult, op1=ALU.mult))
            dve.wait_ge(ex, 2)
            o.seal(nc.vector.tensor_tensor(r, r, lw, ALU.mult))
            dve.wait_ge(ex, 3)
            o.seal(nc.vector.tensor_tensor(k, k, w1, ALU.mult))
            o.seal(nc.vector.tensor_tensor(a, a, w1, ALU.mult))

        @block.scalar
        def _(act):
            act.wait_ge(ss, 1)
            nc.scalar.activation(w0, K.ps[:, :, :], ACT.Sqrt).then_inc(root, 1)
            act.wait_ge(raw, 1)
            nc.scalar.activation(y, lw, ACT.Exp).then_inc(ex, 1)
            act.wait_ge(ex, 1)
            nc.scalar.activation(lw, w1, ACT.Exp).then_inc(ex, 1)
            act.wait_ge(ex, 2)
            nc.scalar.activation(w1, w1, ACT.Exp, scale=-1.0).then_inc(ex, 1)

        @block.tensor
        def _(pe):
            pe.wait_ge(sq, 1)
            head_sums(K, w0).then_inc(ss, 1)
            pe.wait_ge(root, 1)
            pe.wait_ge(rk, KT)
            head_sums(K, w0).then_inc(rks, 1)


LEVELS = (2, 4, 8, 16)


def wkv_chunks(K):
    nc = K.nc
    r, k, v, ec, a, y, kk = (K.slot(n) for n in (S_R, S_K, S_V, S_LW, S_A, S_Y, S_KK))
    G, Q, L = 4, 4, len(LEVELS)

    def taker(region):
        used = [0]

        def take(*shape):
            n = math.prod(shape)
            s = region[:, used[0]:used[0] + n]
            used[0] += n
            if len(shape) == 1:
                return s
            axes = "abc"[:len(shape)]
            return s.rearrange(f"p ({' '.join(axes)}) -> p {' '.join(axes)}", **dict(zip(axes, shape)))
        return take

    take = taker(K.arena[:, S_W1, :])
    ar = take(KT, 2, CH)
    be, ka, vt = take(KT, CH), take(KT, CH), take(KT, CH)
    pc = take(KT, 1)
    st = take(KT, HD)
    rs, us = take(G, HD), take(G, HD)
    yt = take(G, 2, HD)
    take = taker(K.arena[:, S_H, :])
    mt, mak, x, xt, et, yy, mrb, mrk = (take(G, P) for _ in range(8))
    take = taker(K.small)
    cn = take(3, G, HD)
    consts = K.small[:, 768:768 + K.ins["c_wkv"].shape[1]]
    upper, lower = take(Q, CH), take(Q, CH)
    incl = take(Q, CH)
    lev = take(L, P)
    lev0, lev0t = take(Q, CH), take(P)

    pn = K.ps[:, 0:2, :].rearrange("p b (a g i) -> p (b a) g i", a=2, g=G)
    gb = K.ps[:, 2, :].rearrange("p (w g c) -> p w g c", w=2, g=G)
    ga = K.ps[:, 3, 0:G * CH].rearrange("p (g c) -> p g c", g=G)
    pr = K.ps[:, 3, 128:128 + G * HD].rearrange("p (g i) -> p g i", g=G)
    pY, pZ, pZt = (K.ps[:, n, :].rearrange("p (g c) -> p g c", g=G) for n in (4, 5, 6))
    pu = K.ps[:, 4, 0:G * HD].rearrange("p (g i) -> p g i", g=G)
    pyt = K.ps[:, 7, 0:G * HD].rearrange("p (g i) -> p g i", g=G)
    pyf = K.ps[:, 0, :].rearrange("p (g h e t) -> p g h e t", g=G, h=2, e=2)
    pst = K.ps[:, 5:7, 0:G * HD].rearrange("p b (g i) -> p b g i", g=G)
    heads = [(g, q, 2 * g + q // 2, slice(64 * (q % 2), 64 * (q % 2) + 64), slice(32 * q, 32 * q + 32))
             for g in range(G) for q in range(Q)]
    with Stage(nc) as S:
        loaded, zeroed = S.sem("consts_loaded"), S.sem("state_zero")
        pe_s = Steps(S.sem("pe_steps"), ["grams", "token"] + [x for l in range(L) for x in (f"Y{l}", *({0: ["R"], 1: ["y0"]}.get(l, [])), f"Z{l}")]
                     + ["U", "y", "state", "turned"])
        dve_s = Steps(S.sem("dve_steps"), ["rho", "v", "decay", "mt", "x", "xt", "x1", "xt1", "et0", "mak", "mrk", "mrb"]
                      + [f"{z}{l + (z == 'et')}" for l in range(L - 1) for z in ("et", "x_", "xt_")] + [f"x_{L - 1}", "sum", "state"])
        act_s = Steps(S.sem("act_steps"), ["alpha", "beta", "kappa", "token", "token2", "Y0", "R"] + [f"Y{l}" for l in range(1, L)] + ["U", "y", "out0", "out1"])
        first = S.sem("pe_round")
        block = S.block()

        @block.sync
        def _(sp):
            sp.dma_start(consts, K.ins["c_wkv"]).then_inc(loaded, 16)

        @block.vector
        def _(dve):
            nc.vector.memset(st, 0.0).then_inc(zeroed, 1)
            dve.wait_ge(loaded, 16)
            dve.wait_ge(zeroed, 1)
            dve.sem_inc(dve_s.sem, 1)

            def body(i):
                def seal(name, ins):
                    ins.then_inc(dve_s.sem, 1)
                    dve.wait_ge(dve_s.sem, dve_s.at(name, i))

                now = bass.ds(i * CH, CH)
                dve.wait_ge(pe_s.sem, pe_s.before(i))
                nc.vector.tensor_copy(ar[:, :, 1, :], r[:, :, now]).then_inc(dve_s.sem, 1)
                nc.vector.tensor_copy(vt, v[:, :, now]).then_inc(dve_s.sem, 1)
                nc.vector.tensor_copy(pc, ec[:, :, bass.ds(i * CH + (CH - 1), 1)]).then_inc(dve_s.sem, 1)
                dve.wait_ge(pe_s.sem, pe_s.at("grams", i))
                g4 = lambda s: bc(s.unsqueeze(2), [P, G, Q, CH])
                m4 = lambda s: bc(s.unsqueeze(1), [P, G, Q, CH])
                st4 = st.rearrange("p (g b) i -> p b g i", b=2)
                v4 = lambda s: s.rearrange("p g (q t) -> p g q t", q=Q)
                over_g = lambda s, n: bc(s.unsqueeze(1), [P, G, n])
                nc.vector.tensor_tensor(v4(mt), g4(ga), m4(lower), ALU.mult).then_inc(dve_s.sem, 1)
                seal("x", nc.vector.tensor_tensor(v4(x), g4(gb[:, 0, :, 0:CH]), m4(lev0), ALU.mult))
                seal("xt", nc.vector.tensor_tensor(xt, mt, over_g(lev0t, P), ALU.mult))
                nc.vector.tensor_tensor(x, x, over_g(K.ident[:, :], P), ALU.add).then_inc(dve_s.sem, 1)
                nc.vector.tensor_tensor(xt, xt, over_g(K.ident[:, :], P), ALU.add).then_inc(dve_s.sem, 1)
                blocks = lambda l: nc.vector.tensor_tensor(et, mt, over_g(lev[:, l, :], P), ALU.mult).then_inc(dve_s.sem, 1)
                blocks(0)
                nc.vector.tensor_tensor(v4(mak), g4(gb[:, 1, :, 0:CH]), m4(upper), ALU.mult).then_inc(dve_s.sem, 1)
                nc.vector.tensor_tensor(v4(mrk), g4(gb[:, 1, :, CH:]), m4(incl), ALU.mult).then_inc(dve_s.sem, 1)
                nc.vector.tensor_tensor(v4(mrb), g4(gb[:, 0, :, CH:]), m4(incl), ALU.mult).then_inc(dve_s.sem, 1)
                for l in range(L):
                    if l < L - 1:
                        dve.wait_ge(pe_s.sem, pe_s.at(f"Y{l}", i))
                        blocks(l + 1)
                    dve.wait_ge(pe_s.sem, pe_s.at(f"Z{l}", i))
                    seal(f"x_{l}", nc.vector.tensor_tensor(x, x, pZ, ALU.add))
                    if l < L - 1:
                        seal(f"xt_{l}", nc.vector.tensor_tensor(xt, xt, pZt, ALU.add))
                dve.wait_ge(pe_s.sem, pe_s.at("state", i))
                seal("sum", nc.vector.tensor_tensor(st4, st4, pst, ALU.add))
                seal("state", nc.vector.tensor_tensor(st, st, bc(pc, [P, KT, HD]), ALU.mult))
            loop(dve, NC, body)

        @block.scalar
        def _(act):
            act.sem_inc(act_s.sem, 1)

            def body(i):
                now = bass.ds(i * CH, CH)
                act.wait_ge(pe_s.sem, pe_s.before(i))
                nc.scalar.activation(ar[:, :, 0, :], kk[:, :, now], ACT.Copy).then_inc(act_s.sem, 1)
                nc.scalar.activation(be, a[:, :, now], ACT.Copy).then_inc(act_s.sem, 1)
                nc.scalar.activation(ka, k[:, :, now], ACT.Copy).then_inc(act_s.sem, 1)
                act.wait_ge(pe_s.sem, pe_s.at("token", i))
                nc.scalar.activation(cn[:, 0:2], pn[:, 0:2], ACT.Copy).then_inc(act_s.sem, 1)
                nc.scalar.activation(cn[:, 2], pn[:, 2], ACT.Copy).then_inc(act_s.sem, 1)
                for l in range(L):
                    act.wait_ge(pe_s.sem, pe_s.at(f"Y{l}", i))
                    nc.scalar.activation(yy, pY, ACT.Copy).then_inc(act_s.sem, 1)
                    if l == 0:
                        act.wait_ge(pe_s.sem, pe_s.at("R", i))
                        nc.scalar.activation(rs, pr, ACT.Copy).then_inc(act_s.sem, 1)
                act.wait_ge(pe_s.sem, pe_s.at("U", i))
                nc.scalar.activation(us, pu, ACT.Copy).then_inc(act_s.sem, 1)
                act.wait_ge(pe_s.sem, pe_s.at("y", i))
                nc.scalar.activation(yt, bc(pyt.unsqueeze(2), [P, G, 2, HD]), ACT.Copy).then_inc(act_s.sem, 1)
                act.wait_ge(pe_s.sem, pe_s.at("turned", i))
                for e in range(2):
                    half = slice(64 * e, 64 * e + 64)
                    nc.scalar.activation(y[half, :, now].rearrange("p (g h) t -> p g h t", h=2), pyf[half, :, :, e, :],
                                         ACT.Copy).then_inc(act_s.sem, 1)
            loop(act, NC, body)

        @block.tensor
        def _(pe):
            mm = nc.tensor.matmul
            pe.sem_inc(pe_s.sem, 1)

            def body(i):
                pe.wait_ge(dve_s.sem, dve_s.at("decay", i))
                pe.wait_ge(act_s.sem, act_s.at("kappa", i))
                pe.sem_inc(first, 1)
                for g, q, t, f, h in heads:
                    mm(gb[h, 0, g, :], be[f, t, :], ar[f, t, :, :], start=True, stop=True)
                    mm(gb[h, 1, g, :], ka[f, t, :], ar[f, t, :, :], start=True, stop=True)
                    last = mm(ga[h, g, :], ar[f, t, 0, :], be[f, t, :], start=True, stop=True)
                last.then_inc(pe_s.sem, 1)
                for g, q, t, f, h in heads:
                    for j, src in enumerate((vt, be, ka)):
                        last = mm(pn[h, j, g, :], src[f, t, :], K.ident[f, f], start=True, stop=True)
                last.then_inc(pe_s.sem, 1)
                for l in range(L):
                    pe.wait_ge(dve_s.sem, dve_s.at(f"x_{l - 1}", i) if l else dve_s.at("et0", i))
                    for g in range(G):
                        last = mm(pY[:, g, :], et[:, g, :], x[:, g, :], start=True, stop=True)
                    last.then_inc(pe_s.sem, 1)
                    if l == 0:
                        pe.wait_ge(act_s.sem, act_s.at("token2", i))
                        pe.wait_ge(dve_s.sem, dve_s.at("mak", i))
                        for g in range(G):
                            mm(pr[:, g, :], mak[:, g, :], cn[:, 0, g, :], start=True, stop=False, skip_group_check=True)
                            for _, q, t, f, h in heads[4 * g:4 * g + 4]:
                                last = mm(pr[h, g, :], ar[f, t, 0, :], st[f, t, :], start=False, stop=(q == 3), skip_group_check=True)
                        last.then_inc(pe_s.sem, 1)
                    if l == 1:
                        for g in range(G):
                            mm(pyt[:, g, :], mrk[:, g, :], cn[:, 0, g, :], start=(g == 0), stop=False, skip_group_check=True)
                            for _, q, t, f, h in heads[4 * g:4 * g + 4]:
                                last = mm(pyt[h, g, :], ar[f, t, 1, :], st[f, t, :], start=False, stop=False, skip_group_check=True)
                        last.then_inc(pe_s.sem, 1)
                    pe.wait_ge(act_s.sem, act_s.at(f"Y{l}", i))
                    if l:
                        pe.wait_ge(dve_s.sem, dve_s.at(f"xt_{l - 1}", i))
                    for g in range(G):
                        last = mm(pZ[:, g, :], xt[:, g, :], yy[:, g, :], start=True, stop=True)
                        if l < L - 1:
                            last = mm(pZt[:, g, :], yy[:, g, :], xt[:, g, :], start=True, stop=True)
                    last.then_inc(pe_s.sem, 1)
                pe.wait_ge(act_s.sem, act_s.at("R", i))
                pe.wait_ge(dve_s.sem, dve_s.at(f"x_{L - 1}", i))
                for g in range(G):
                    last = mm(pu[:, g, :], x[:, g, :], rs[:, g, :], start=True, stop=True)
                last.then_inc(pe_s.sem, 1)
                pe.wait_ge(act_s.sem, act_s.at("U", i))
                for g in range(G):
                    last = mm(pyt[:, g, :], mrb[:, g, :], us[:, g, :], start=False, stop=True, skip_group_check=True)
                last.then_inc(pe_s.sem, 1)
                for g, q, t, f, h in heads:
                    mm(pst[f, t % 2, g, :], cn[h, 1, g, :], us[h, g, :], start=True, stop=False, skip_group_check=True)
                    last = mm(pst[f, t % 2, g, :], cn[h, 2, g, :], cn[h, 0, g, :], start=False, stop=True, skip_group_check=True)
                last.then_inc(pe_s.sem, 1)
                pe.wait_ge(act_s.sem, act_s.at("y", i))
                for g in range(G):
                    last = mm(pyf[:, g, :, :, :], yt[:, g, :, :], K.ident[:, :], start=True, stop=True)
                last.then_inc(pe_s.sem, 1)
            loop(pe, NC, body)


def wkv_constants(np):
    p = np.arange(P)
    same = (p[:, None] // CH) == (p[None, :] // CH)
    up = same & (p[:, None] < p[None, :])

    def level(b):
        return up & (p[:, None] // (2 * b) == p[None, :] // (2 * b)) & (p[:, None] // b != p[None, :] // b)
    incl = same & (p[:, None] <= p[None, :])
    parts = [up, up.T, incl] + [level(b).T for b in LEVELS] + [level(1), level(1).T]
    return np.concatenate([np.asarray(x, np.float32) for x in parts], axis=1)


def dump(K, name, src):
    with Stage(K.nc) as S:
        stored = S.sem("stored")
        block = S.block()

        @block.sync
        def _(sp):
            sp.dma_start(K.ins[name], src).then_inc(stored, 16)
            sp.wait_ge(stored, 16)


def residual(K, y, gate, x, z):
    nc = K.nc
    with Stage(nc) as S:
        gated, summed = S.sem("gated"), S.sem("summed")
        block = S.block()

        @block.scalar
        def _(act):
            for k in range(KT):
                nc.scalar.activation(y[:, k, :], y[:, k, :], ACT.Copy, scale=gate(k)).then_inc(gated, 1)

        @block.vector
        def _(dve):
            for k in range(KT):
                dve.wait_ge(gated, k + 1)
                nc.vector.scalar_tensor_tensor(out=z[:, k, :], in0=x[:, k, :], scalar=ALPHA, in1=y[:, k, :],
                                               op0=ALU.mult, op1=ALU.add).then_inc(summed, 1)


def layer_norm(K, l, j, z, tmp, x):
    normalise(K, z, x, tmp, K.mean[:, :], 1.0, K.v("eps_ln"), True,
              lambda k: K.v("ln_g", (2 * l + j) * KT + k), lambda k: K.v("ln_b", (2 * l + j) * KT + k))


def rwkv_layer(K):
    nc = K.nc
    X, H = K.slot(S_X), K.slot(S_H)
    mod = K.mod[0]
    scale_shift(K, X, H, lambda k: mod[:, 8 + k:9 + k], lambda k: mod[:, k:k + 1])

    def difference(dve, o):
        xx = K.slot(S_KK)
        o.seal(nc.vector.tensor_tensor(xx[:, :, 1:], H[:, :, :T - 1], H[:, :, 1:], ALU.subtract))
        o.seal(nc.vector.tensor_scalar(xx[:, :, 0:1], H[:, :, 0:1], -1.0, None, ALU.mult))
    vector_stage(K, difference)
    for n, (mix, dst) in enumerate(((0, S_R), (2, S_K), (3, S_V))):
        linear(K, K.ins["rw_rkv"][0, n], D, K.slot(S_Y), to_slot(nc, K.slot(dst)), wslot=S_W0,
               pre=mixed(K, mix, K.slot(S_Y)), n_pre=KT)
    lora(K, 1, K.ins["rw_w1"][0], K.ins["rw_w2"][0], 64, ACT.Tanh, ACT.Sigmoid, "w0", K.slot(S_LW))
    lora(K, 4, K.ins["rw_a1"][0], K.ins["rw_a2"][0], 64, ACT.Copy, ACT.Sigmoid, "a0", K.slot(S_A))
    lora(K, 5, K.ins["rw_g1"][0], K.ins["rw_g2"][0], 160, ACT.Sigmoid, ACT.Copy, None, K.slot(S_G))
    wkv_inputs(K)
    wkv_chunks(K)
    Y = K.slot(S_Y)
    normalise(K, Y, Y, K.slot(S_R), K.blk[:, :], 1.0 / HD, K.v("eps_gn"), True,
              lambda k: K.v("gn_g", k), lambda k: K.v("gn_b", k), per_tile=True)

    def gated(dve, o):
        o.seal(nc.vector.tensor_tensor(Y, Y, K.slot(S_W0), ALU.add))
        o.seal(nc.vector.tensor_tensor(Y, Y, K.slot(S_G), ALU.mult))
    vector_stage(K, gated)
    linear(K, K.ins["rw_wo"][0], D, Y, to_slot(nc, K.slot(S_R)), wslot=S_W0)



def first_of_largest(K, o, x, n, scratch, onehot, largest):
    v = K.nc.vector
    tie, low = scratch[:, 0:TT * n].rearrange("p (t n) -> p t n", n=n), scratch[:, TT * n:TT * n + TT]
    o.seal(v.tensor_reduce(largest, x, AX.X, ALU.max))
    o.seal(v.tensor_tensor(tie, x, bc(largest.unsqueeze(2), [P, TT, n]), ALU.is_equal))
    o.seal(v.tensor_tensor(tie, tie, bc(K.vs("places")[:, 0:n].unsqueeze(1), [P, TT, n]), ALU.mult))
    o.seal(v.tensor_reduce(low, tie, AX.X, ALU.min))
    o.seal(v.tensor_tensor(onehot, tie, bc(low.unsqueeze(2), [P, TT, n]), ALU.is_equal))


def route_groups(K, l):
    nc = K.nc
    v = nc.vector
    h = K.slot(S_H)
    n = NG + NE
    used = [0]

    def take(*shape):
        m = math.prod(shape)
        s = K.small[:, used[0]:used[0] + m]
        used[0] += m
        return s if len(shape) == 1 else s.rearrange("p (t n) -> p t n", n=shape[1])
    wr, bias = take(KT, n), take(n)
    lg = take(TT, n)
    gates, place = K.gates[:, :, 0:NE], K.places[:, :, 0:NE]
    ohg, dg = take(TT, NG), take(TT, NG)
    el, oh1, oh2, el2 = (take(TT, EPG) for _ in range(4))
    prod, scratch = take(TT, NE), take(TT * EPG + TT)
    mg, z, pg, m1, m2, e2, g1, g2 = (take(TT) for _ in range(8))
    chose = take(TT, NE)
    tri = K.at(40, 1)[:, 0, 0:2 * P].rearrange("p (d t) -> p d t", d=2)
    incl = K.ps[:, 1, 0:TT * NE].rearrange("p (t n) -> p t n", n=NE)
    with Stage(nc) as S:
        loaded, logits, shifted, expd, chosen, counted, fullest, turned, own = (S.sem(x) for x in (
            "loaded", "logits", "shifted", "exps", "chosen", "counted", "fullest", "turned", "own"))
        block = S.block()

        @block.sync
        def _(sp):
            sp.dma_start(wr[:, :, 0:NG], K.ins["moe_wgrp"][l].rearrange("(k p) n -> p k n", p=P)).then_inc(loaded, 16)
            sp.dma_start(wr[:, :, NG:n], K.ins["moe_wexp"][l].rearrange("(k p) n -> p k n", p=P)).then_inc(loaded, 16)
            sp.dma_start(bias[:, 0:NG], K.ins["moe_bgrp"][l:l + 1, :].broadcast_to([P, NG])).then_inc(loaded, 16)
            sp.dma_start(bias[:, NG:n], K.ins["moe_bexp"][l:l + 1, :].broadcast_to([P, NE])).then_inc(loaded, 16)
            sp.dma_start(tri, K.ins["c_tri"]).then_inc(loaded, 16)

        @block.tensor
        def _(pe):
            pe.wait_ge(loaded, 80)
            for t in range(TT):
                for k in range(KT):
                    mm = nc.tensor.matmul(K.ps[:, 0, t * n:(t + 1) * n], h[:, k, t * P:(t + 1) * P], wr[:, k, :],
                                          start=(k == 0), stop=(k == KT - 1))
            mm.then_inc(logits, 1)
            pe.wait_ge(chosen, 1)
            for t in range(TT):
                for u in range(t + 1):
                    mm = nc.tensor.matmul(incl[:, t, :], tri[:, 0, :] if u == t else K.ones[:, :], chose[:, u, :],
                                          start=(u == 0), stop=(u == t))
            mm.then_inc(counted, 1)
            pe.wait_ge(fullest, 1)
            nc.tensor.transpose(K.ps[0:1, 2, 0:P], z[:, 0:1], K.ident[:, :]).then_inc(turned, 1)

        @block.vector
        def _(dve):
            o = Own(dve, own)
            dve.wait_ge(logits, 1)
            o.seal(v.tensor_tensor(lg, K.ps[:, 0, 0:TT * n].rearrange("p (t n) -> p t n", n=n),
                                   bc(bias.unsqueeze(1), [P, TT, n]), ALU.add))
            first_of_largest(K, o, lg[:, :, 0:NG], NG, scratch, ohg, mg)
            v.tensor_tensor(dg, lg[:, :, 0:NG], bc(mg.unsqueeze(2), [P, TT, NG]), ALU.subtract).then_inc(shifted, 1)
            pr4 = prod.rearrange("p t (g j) -> p t g j", g=NG)
            o.seal(v.tensor_tensor(pr4, lg[:, :, NG:n].rearrange("p t (g j) -> p t g j", g=NG),
                                   bc(ohg.unsqueeze(3), [P, TT, NG, EPG]), ALU.mult))
            o.seal(v.tensor_reduce(el, prod.rearrange("p t (g j) -> p t j g", g=NG), AX.X, ALU.add))
            first_of_largest(K, o, el, EPG, scratch, oh1, m1)
            o.seal(v.scalar_tensor_tensor(out=el2, in0=oh1, scalar=-1e30, in1=el, op0=ALU.mult, op1=ALU.add))
            first_of_largest(K, o, el2, EPG, scratch, oh2, m2)
            v.tensor_tensor(m2, m2, m1, ALU.subtract).then_inc(shifted, 1)
            dve.wait_ge(expd, 1)
            o.seal(v.tensor_reduce(z, dg, AX.X, ALU.add))
            o.seal(v.reciprocal(pg, z))
            dve.wait_ge(expd, 2)
            o.seal(v.tensor_scalar(g2, e2, 1.0, None, ALU.add))
            o.seal(v.reciprocal(g2, g2))
            o.seal(v.tensor_tensor(g1, pg, g2, ALU.mult))
            o.seal(v.tensor_tensor(g2, g1, e2, ALU.mult))
            o.seal(v.tensor_tensor(el2, oh1, oh2, ALU.add))
            v.tensor_tensor(chose.rearrange("p t (g j) -> p t g j", g=NG), bc(el2.unsqueeze(2), [P, TT, NG, EPG]),
                            bc(ohg.unsqueeze(3), [P, TT, NG, EPG]), ALU.mult).then_inc(chosen, 1)
            o.seal(v.tensor_tensor(oh1, oh1, bc(g1.unsqueeze(2), [P, TT, EPG]), ALU.mult))
            o.seal(v.tensor_tensor(oh2, oh2, bc(g2.unsqueeze(2), [P, TT, EPG]), ALU.mult))
            o.seal(v.tensor_tensor(oh1, oh1, oh2, ALU.add))
            o.seal(v.tensor_tensor(gates.rearrange("p t (g j) -> p t g j", g=NG), bc(oh1.unsqueeze(2), [P, TT, NG, EPG]),
                                   bc(ohg.unsqueeze(3), [P, TT, NG, EPG]), ALU.mult))
            o.seal(v.memset(K.places[:, :, NE:], -1.0))
            dve.wait_ge(counted, 1)
            dve.wait_ge(chosen, 1)
            o.seal(v.tensor_tensor(place, incl, chose, ALU.mult))
            o.seal(v.tensor_reduce(z, place, AX.X, ALU.max))
            o.seal(v.tensor_scalar(place, place, -1.0, None, ALU.add))
            v.tensor_reduce(z[:, 0:1], z, AX.X, ALU.max).then_inc(fullest, 1)
            dve.wait_ge(turned, 1)
            o.seal(v.tensor_reduce(z[0:1, 1:2], K.ps[0:1, 2, 0:P], AX.X, ALU.max))
            o.seal(v.tensor_scalar(z[0:1, 1:2], z[0:1, 1:2], float(SEATS), None, ALU.is_gt))
            o.seal(v.tensor_copy(K.crowded, z[0:1, 1:2]))

        @block.scalar
        def _(act):
            act.wait_ge(shifted, 1)
            nc.scalar.activation(dg, dg, ACT.Exp).then_inc(expd, 1)
            act.wait_ge(shifted, 2)
            nc.scalar.activation(e2, m2, ACT.Exp).then_inc(expd, 1)


def route_tokens(K):
    nc = K.nc
    v = nc.vector
    h = K.slot(S_H)
    wr = K.small[:, 0:KT * NE2].rearrange("p (k n) -> p k n", n=NE2)
    lg = K.small[:, 128:128 + TT * NE2].rearrange("p (t n) -> p t n", n=NE2)
    mx, z = K.small[:, 192:192 + TT], K.small[:, 200:200 + TT]
    top = K.small[0:NE2, 208:216]
    aff, left, one, place = (K.at(16 + j, 1)[0:NE2, 0, :] for j in range(4))
    col = lambda j: K.ps[:, 2, 64 * j:64 * j + 64].rearrange("p (t n) -> p t n", n=NE2)
    with Stage(nc) as S:
        loaded, logits, shifted, expd, made, turned, chosen, stored, own = (S.sem(x) for x in (
            "loaded", "logits", "shifted", "exps", "affinities", "turned", "chosen", "unused", "own"))
        block = S.block()

        @block.sync
        def _(sp):
            sp.dma_start(wr, K.ins["w_router_2"][0].rearrange("(k p) n -> p k n", p=P)).then_inc(loaded, 16)

        @block.tensor
        def _(pe):
            pe.wait_ge(loaded, 16)
            for t in range(TT):
                for k in range(KT):
                    mm = nc.tensor.matmul(K.ps[:, 0, t * NE2:(t + 1) * NE2], h[:, k, t * P:(t + 1) * P], wr[:, k, :],
                                          start=(k == 0), stop=(k == KT - 1))
            mm.then_inc(logits, 1)
            pe.wait_ge(made, 1)
            for t in range(TT):
                mm = nc.tensor.transpose(K.ps[0:NE2, 1, t * P:(t + 1) * P], lg[:, t, :], K.ident[:, :])
            mm.then_inc(turned, 1)
            pe.wait_ge(chosen, 1)
            for j, src in enumerate((left, place)):
                for t in range(TT):
                    mm = nc.tensor.transpose(col(j)[:, t, :], src[:, t * P:(t + 1) * P], K.ident[0:NE2, 0:NE2])
            mm.then_inc(turned, 1)

        @block.vector
        def _(dve):
            o = Own(dve, own)
            dve.wait_ge(logits, 1)
            src = K.ps[:, 0, 0:TT * NE2].rearrange("p (t n) -> p t n", n=NE2)
            o.seal(v.tensor_reduce(mx, src, AX.X, ALU.max))
            v.tensor_tensor(lg, src, bc(mx.unsqueeze(2), [P, TT, NE2]), ALU.subtract).then_inc(shifted, 1)
            dve.wait_ge(expd, 1)
            o.seal(v.tensor_reduce(z, lg, AX.X, ALU.add))
            o.seal(v.reciprocal(z, z))
            v.tensor_tensor(lg, lg, bc(z.unsqueeze(2), [P, TT, NE2]), ALU.mult).then_inc(made, 1)
            dve.wait_ge(turned, 1)
            o.seal(v.tensor_copy(aff, K.ps[0:NE2, 1, :]))
            o.seal(v.tensor_copy(left, aff))
            for _ in range(CAP // 8):
                o.seal(v.max(top, left))
                o.seal(v.match_replace(left, top, left, -1.0))
            o.seal(v.tensor_scalar(left, left, 0.0, None, ALU.is_lt))
            o.seal(v.memset(one, 1.0))
            o.seal(v.tensor_tensor_scan(place, one, left, 0.0, ALU.mult, ALU.add))
            o.seal(v.tensor_tensor(place, place, left, ALU.mult))
            o.seal(v.tensor_scalar(place, place, -1.0, None, ALU.add))
            v.tensor_tensor(left, left, aff, ALU.mult).then_inc(chosen, 1)
            o.seal(v.memset(K.places[:, :, NE2:], -1.0))
            dve.wait_ge(turned, 2)
            o.seal(v.tensor_copy(K.gates[:, :, 0:NE2], col(0)))
            o.seal(v.tensor_copy(K.places[:, :, 0:NE2], col(1)))

        @block.scalar
        def _(act):
            act.wait_ge(shifted, 1)
            nc.scalar.activation(lg, lg, ACT.Exp).then_inc(expd, 1)


def all_tokens_experts(K, crowded, n, wg, wu, wd):
    nc = K.nc
    h, acc = K.slot(S_H), K.slot(2)
    hid = K.at(24, 4)
    grow = K.at(28, 2)
    sg = K.at(30, 2)
    FTL = DE // P
    W = [[K.slot(6 + 3 * b + j) for j in range(3)] for b in range(2)]
    with Stage(nc) as S:
        w_in = S.sems("weights_in", 2)
        pe_s = Steps(S.sem("pe_steps"), [f"up{m}" for m in range(FTL)] + [f"down{d}" for d in range(KT)], lead=1)
        act_s = Steps(S.sem("act_steps"), [f"silu{m}" for m in range(FTL)], lead=1)
        dve_s = Steps(S.sem("dve_steps"), [x for m in range(FTL) for x in (f"gated{m}", f"hid{m}")] + [f"acc{d}" for d in range(KT)], lead=1)
        block = S.block()
        rounds = lambda eng, one: loop(eng, n // 2, lambda i: [one(i, b, i * 2 + b) for b in range(2)])

        @block.sync
        def _(sp):
            with sp.If(crowded > 0):
                def one(i, b, e):
                    sp.wait_ge(pe_s.sem, pe_s.before(e - 1))
                    sp.wait_ge(dve_s.sem, dve_s.before(e - 1))
                    for j, src in enumerate((wg(i, b), wu(i, b), wd(i, b))):
                        dst = W[b][j] if j < 2 else W[b][j].rearrange("p k t -> p (k t)").rearrange("p (k t) -> p k t", t=D)
                        sp.dma_start(dst, src.rearrange("(k p) n -> p k n", p=P)).then_inc(w_in[b], 16)
                    sp.dma_start(grow[:, b, :], K.ins["gates"][bass.ds(i * 2 + b, 1), :].broadcast_to([P, T])).then_inc(w_in[b], 16)
                rounds(sp, one)

        @block.tensor
        def _(pe):
            with pe.If(crowded > 0):
                pe.sem_inc(pe_s.sem, pe_s.base)

                def one(i, b, e):
                    pe.wait_ge(w_in[b], i * 64 + 64)
                    for m in range(FTL):
                        pe.wait_ge(dve_s.sem, dve_s.at(f"hid{m - 2}", e) if m >= 2 else dve_s.at(f"hid{m + 2}", e - 1))
                        for j in range(2):
                            for k in range(KT):
                                mm = nc.tensor.matmul(K.ps[:, 2 * (m % 2) + j, :], W[b][j][:, k, m * P:(m + 1) * P], h[:, k, :],
                                                      start=(k == 0), stop=(k == KT - 1))
                        mm.then_inc(pe_s.sem, 1)
                    wdn = W[b][2].rearrange("p k t -> p (k t)").rearrange("p (k t) -> p k t", t=D)
                    for d in range(KT):
                        pe.wait_ge(dve_s.sem, dve_s.at(f"acc{d - 4}", e) if d >= 4 else dve_s.at(f"hid{FTL - 1}", e))
                        for k in range(FTL):
                            mm = nc.tensor.matmul(K.ps[:, 4 + d % 4, :], wdn[:, k, d * P:(d + 1) * P], hid[:, k, :],
                                                  start=(k == 0), stop=(k == FTL - 1))
                        mm.then_inc(pe_s.sem, 1)
                rounds(pe, one)

        @block.scalar
        def _(act):
            with act.If(crowded > 0):
                act.sem_inc(act_s.sem, act_s.base)

                def one(i, b, e):
                    for m in range(FTL):
                        act.wait_ge(pe_s.sem, pe_s.at(f"up{m}", e))
                        act.wait_ge(dve_s.sem, dve_s.at(f"hid{m - 2}", e) if m >= 2 else dve_s.at(f"hid{m + 2}", e - 1))
                        nc.scalar.activation(sg[:, m % 2, :], K.ps[:, 2 * (m % 2), :], ACT.Silu).then_inc(act_s.sem, 1)
                rounds(act, one)

        @block.vector
        def _(dve):
            with dve.If(crowded > 0):
                dve.sem_inc(dve_s.sem, dve_s.base)

                def one(i, b, e):
                    dve.wait_ge(w_in[b], i * 64 + 64)
                    for m in range(FTL):
                        dve.wait_ge(act_s.sem, act_s.at(f"silu{m}", e))
                        nc.vector.tensor_tensor(sg[:, m % 2, :], sg[:, m % 2, :], grow[:, b, :], ALU.mult).then_inc(dve_s.sem, 1)
                        dve.wait_ge(dve_s.sem, dve_s.at(f"gated{m}", e))
                        if m == 0:
                            dve.wait_ge(pe_s.sem, pe_s.before(e))
                        nc.vector.tensor_tensor(hid[:, m, :], sg[:, m % 2, :], K.ps[:, 2 * (m % 2) + 1, :], ALU.mult).then_inc(dve_s.sem, 1)
                    for d in range(KT):
                        dve.wait_ge(pe_s.sem, pe_s.at(f"down{d}", e))
                        nc.vector.tensor_tensor(acc[:, d, :], acc[:, d, :], K.ps[:, 4 + d % 4, :], ALU.add).then_inc(dve_s.sem, 1)
                rounds(dve, one)


def token_form(K):
    nc = K.nc
    h, hn = K.slot(S_H), K.arena[:, 3, :].rearrange("p (t d) -> p t d", t=TT)
    parts = [(t, q) for t in range(TT) for q in range(2)]
    with Stage(nc) as S:
        turned, taken = S.sem("turned"), S.sem("taken")
        block = S.block()

        @block.tensor
        def _(pe):
            for m, (t, q) in enumerate(parts):
                for j in range(4):
                    mm = nc.tensor.transpose(K.ps[:, m, j * P:(j + 1) * P], h[:, 4 * q + j, t * P:(t + 1) * P], K.ident[:, :])
                mm.then_inc(turned, 1)

        @block.scalar
        def _(act):
            for m, (t, q) in enumerate(parts):
                act.wait_ge(turned, m + 1)
                nc.scalar.activation(hn[:, t, q * 512:(q + 1) * 512], K.ps[:, m, :], ACT.Copy).then_inc(taken, 1)


def experts(K, n, H, wg, wu, wd):
    nc = K.nc
    SL = 2 * SEATS
    FTL = DE // P
    hn = K.arena[:, 3, :].rearrange("p (t d) -> p t d", t=TT)
    acc = K.slot(2)
    xg = K.flat(32, KT * SL).rearrange("p (k s) -> p k s", k=KT)
    xrow = K.flat(34, D)
    yrow = K.flat(36, D)
    hid, sg = K.flat(38, DE), K.flat(39, DE)
    back = K.flat(40, T)
    take = K.flat(41, TT * SL).rearrange("p (t s) -> p t s", t=TT)
    give = K.flat(42, TT * SL).rearrange("p (t s) -> p t s", t=TT)
    seats = K.flat(43, SEATS)
    hidT = K.flat(44, DE).rearrange("p (k s) -> p k s", k=FTL)
    nxt, now, gate = (K.small[:, 2400 + 8 * j:2408 + 8 * j].rearrange("p (t b) -> p t b", b=2) for j in range(3))
    W = [[K.slot(6 + 3 * b + j) for j in range(3)] for b in range(2)]
    down = [w[2].rearrange("p k t -> p (k t)").rearrange("p (k t) -> p k t", t=D) for w in W]
    half = [slice(b * SEATS, (b + 1) * SEATS) for b in range(2)]
    bank = lambda b: K.ps[:, b, :]
    parts = range(H)
    backs = [f"back{d}" for d in range(KT)]
    pe_names, act_names, dve_names = [], [], ["next", "now", "gate", "take", "give"]
    for c in parts:
        pe_names += [f"upA{c}", f"upB{c}"] + (backs if c == 0 else []) + (["gather"] if c == H - 1 else []) + [f"hid{c}"]
        pe_names += (["gates", "x"] if c == H - 1 else []) + [f"downA{c}", f"downB{c}"]
        act_names += [f"silu{c}"] + (["row0", "row1"] if c == H - 1 else []) + [f"hid{c}"]
        dve_names += [f"hid{c}"] + ([f"acc{d}" for d in range(KT)] if c == 0 else [])
    act_names += ["gates", "x0", "x1", "y0", "y1"]
    with Stage(nc) as S:
        w_in = [S.sems(f"weights{b}_in", 3) for b in range(2)]
        loaded, zeroed, rounds = S.sem("seats_loaded"), S.sem("zeroed"), S.sem("pe_rounds")
        pe_s = Steps(S.sem("pe_steps"), pe_names, lead=1)
        act_s = Steps(S.sem("act_steps"), act_names, lead=1)
        dve_s = Steps(S.sem("dve_steps"), dve_names, lead=1)
        block = S.block()

        @block.sync
        def _(sp):
            sp.dma_start(seats, K.ins["c_seats"]).then_inc(loaded, 16)

            def one(i):
                for c in parts:
                    last = lambda name: pe_s.at(f"{name}{c - 1}", i) if c else pe_s.at(f"{name}{H - 1}", i - 1)
                    for b, x in enumerate("AB"):
                        sp.wait_ge(pe_s.sem, last(f"up{x}"))
                        sp.dma_start(W[b][0], wg(i, b, c).rearrange("(k p) n -> p k n", p=P)).then_inc(w_in[b][0], 16)
                        sp.dma_start(W[b][1], wu(i, b, c).rearrange("(k p) n -> p k n", p=P)).then_inc(w_in[b][1], 16)
                    for b, x in enumerate("AB"):
                        sp.wait_ge(pe_s.sem, last(f"down{x}"))
                        sp.dma_start(down[b], wd(i, b, c).rearrange("(k p) n -> p k n", p=P)).then_inc(w_in[b][2], 16)
            loop(sp, n, one)

        @block.tensor
        def _(pe):
            mm = nc.tensor.matmul

            def gather():
                for q in range(2):
                    for t in range(TT):
                        last = mm(bank(2 + q), take[:, t, :], hn[:, t, q * 512:(q + 1) * 512], start=(t == 0), stop=(t == TT - 1))
                return last

            def turn_rows():
                for k in range(KT):
                    last = nc.tensor.transpose(K.ps[:, 2 + k // 4, (k % 4) * P:(k % 4 + 1) * P], xrow[:, k * P:(k + 1) * P], K.ident[:, :])
                return last

            def give_back(d):
                mm(bank(6 + d % 2), yrow[:, d * P:(d + 1) * P], back, start=True, stop=True).then_inc(pe_s.sem, 1)

            pe.wait_ge(dve_s.sem, dve_s.before(0))
            pe.sem_inc(pe_s.sem, pe_s.at("gather", -1) - 1)
            gather().then_inc(pe_s.sem, 1)
            pe.wait_ge(act_s.sem, act_s.at("row1", -1))
            turn_rows().then_inc(pe_s.sem, pe_s.before(0) - pe_s.at("gather", -1))

            def one(i):
                pe.wait_ge(act_s.sem, act_s.at("x1", i - 1))
                for c in parts:
                    if c:
                        pe.wait_ge(act_s.sem, act_s.at(f"hid{c - 1}", i))
                    for b, x in enumerate("AB"):
                        for j in range(2):
                            pe.wait_ge(w_in[b][j], (i * H + c) * 16 + 16)
                            pe.sem_inc(rounds, 1)
                            for k in range(KT):
                                last = mm(K.ps[half[b], j, :], xg[:, k, half[b]], W[b][j][:, k, :], start=(k == 0), stop=(k == KT - 1))
                        last.then_inc(pe_s.sem, 1)
                    if c == 0:
                        pe.wait_ge(act_s.sem, act_s.before(i))
                        for d in range(KT):
                            pe.wait_ge(dve_s.sem, dve_s.at(f"acc{d - 2}", i) if d >= 2 else dve_s.at(f"acc{d + 6}", i - 1))
                            give_back(d)
                    if c == H - 1:
                        pe.wait_ge(dve_s.sem, dve_s.at("take", i))
                        gather().then_inc(pe_s.sem, 1)
                    pe.wait_ge(dve_s.sem, dve_s.at(f"hid{c}", i))
                    pe.sem_inc(rounds, 1)
                    for k in range(FTL):
                        last = nc.tensor.transpose(K.ps[:, 0, k * P:(k + 1) * P], hid[:, k * P:(k + 1) * P], K.ident[:, :])
                    last.then_inc(pe_s.sem, 1)
                    if c == H - 1:
                        for t in range(TT):
                            last = nc.tensor.transpose(K.ps[:, 1, t * P:(t + 1) * P], give[:, t, :], K.ident[:, :])
                        last.then_inc(pe_s.sem, 1)
                        pe.wait_ge(act_s.sem, act_s.at("row1", i))
                        pe.sem_inc(rounds, 1)
                        turn_rows().then_inc(pe_s.sem, 1)
                    pe.wait_ge(act_s.sem, act_s.at(f"hid{c}", i))
                    for b, x in enumerate("AB"):
                        pe.wait_ge(w_in[b][2], (i * H + c) * 16 + 16)
                        pe.sem_inc(rounds, 1)
                        for q in range(2):
                            for k in range(FTL):
                                last = mm(K.ps[half[b], 4 + q, :], hidT[:, k, half[b]], down[b][:, k, q * 512:(q + 1) * 512],
                                          start=(c == k == 0), stop=(c == H - 1 and k == FTL - 1))
                        last.then_inc(pe_s.sem, 1)
            loop(pe, n, one)
            pe.wait_ge(act_s.sem, act_s.before(n))
            for d in range(KT):
                pe.wait_ge(dve_s.sem, dve_s.before(n) + max(d - 1, 0))
                give_back(d)

        @block.scalar
        def _(act):
            copy = lambda dst, src: nc.scalar.activation(dst, src, ACT.Copy)
            cols = lambda q: xg.rearrange("p k s -> p (k s)")[:, q * 512:(q + 1) * 512]

            act.wait_ge(zeroed, 3)
            act.sem_inc(act_s.sem, act_s.at("row0", -1) - 1)
            act.wait_ge(pe_s.sem, pe_s.at("gather", -1))
            for q in range(2):
                copy(xrow[:, q * 512:(q + 1) * 512], bank(2 + q)).then_inc(act_s.sem, 1)
            act.wait_ge(pe_s.sem, pe_s.before(0))
            copy(cols(0), bank(2)).then_inc(act_s.sem, 3)
            copy(cols(1), bank(3)).then_inc(act_s.sem, 3)

            def one(i):
                for c in parts:
                    act.wait_ge(pe_s.sem, pe_s.at(f"upB{c}", i))
                    nc.scalar.activation(sg, bank(0), ACT.Silu).then_inc(act_s.sem, 1)
                    if c == H - 1:
                        act.wait_ge(pe_s.sem, pe_s.at("gather", i))
                        for q in range(2):
                            copy(xrow[:, q * 512:(q + 1) * 512], bank(2 + q)).then_inc(act_s.sem, 1)
                    act.wait_ge(pe_s.sem, pe_s.at(f"hid{c}", i))
                    copy(hidT.rearrange("p k s -> p (k s)"), bank(0)).then_inc(act_s.sem, 1)
                act.wait_ge(pe_s.sem, pe_s.at("gates", i))
                copy(back, bank(1)).then_inc(act_s.sem, 1)
                act.wait_ge(pe_s.sem, pe_s.at("x", i))
                for q in range(2):
                    copy(cols(q), bank(2 + q)).then_inc(act_s.sem, 1)
                act.wait_ge(pe_s.sem, pe_s.at(f"downB{H - 1}", i))
                for q in range(2):
                    copy(yrow[:, q * 512:(q + 1) * 512], bank(4 + q)).then_inc(act_s.sem, 1)
            loop(act, n, one)

        @block.vector
        def _(dve):
            v = nc.vector

            def take_seats(src):
                for t in range(TT):
                    for b in range(2):
                        last = v.tensor_scalar(take[:, t, half[b]], seats, src[:, t, b:b + 1], None, ALU.is_equal)
                return last

            dve.wait_ge(loaded, 16)
            v.memset(acc, 0.0).then_inc(zeroed, 1)
            v.memset(yrow, 0.0).then_inc(zeroed, 1)
            v.memset(back, 0.0).then_inc(zeroed, 1)
            dve.wait_ge(zeroed, 3)
            take_seats(K.places[:, :, 0:2]).then_inc(dve_s.sem, dve_s.base)

            def one(i):
                v.tensor_copy(nxt, K.places[:, :, bass.ds(i * 2 + 2, 2)]).then_inc(dve_s.sem, 1)
                v.tensor_copy(now, K.places[:, :, bass.ds(i * 2, 2)]).then_inc(dve_s.sem, 1)
                v.tensor_copy(gate, K.gates[:, :, bass.ds(i * 2, 2)]).then_inc(dve_s.sem, 1)
                dve.wait_ge(pe_s.sem, pe_s.before(i))
                dve.wait_ge(dve_s.sem, dve_s.at("gate", i))
                take_seats(nxt).then_inc(dve_s.sem, 1)
                for t in range(TT):
                    for b in range(2):
                        last = v.tensor_scalar(give[:, t, half[b]], seats, now[:, t, b:b + 1],
                                               gate[:, t, b:b + 1], ALU.is_equal, ALU.mult)
                last.then_inc(dve_s.sem, 1)
                for c in parts:
                    dve.wait_ge(act_s.sem, act_s.at(f"silu{c}", i))
                    v.tensor_tensor(hid, sg, bank(1), ALU.mult).then_inc(dve_s.sem, 1)
                    if c == 0:
                        for d in range(KT):
                            dve.wait_ge(pe_s.sem, pe_s.at(f"back{d}", i))
                            v.tensor_tensor(acc[:, d, :], acc[:, d, :], bank(6 + d % 2), ALU.add).then_inc(dve_s.sem, 1)
            loop(dve, n, one)
            for d in range(KT):
                dve.wait_ge(pe_s.sem, pe_s.before(n) + d + 1)
                v.tensor_tensor(acc[:, d, :], acc[:, d, :], bank(6 + d % 2), ALU.add).then_inc(dve_s.sem, 1)


def seatless(K, pick):
    nc = K.nc
    working = set(mybir.ALL_ENGINES) - {mybir.EngineType.Pool}
    crowded = nc.values_load(K.crowded, engines=working, min_val=0, max_val=1)
    rest = K.at(40, 1)[:, 0, 0:TT * NE].rearrange("p (t n) -> p t n", n=NE)
    rows = K.at(41, 1)[0:NE, 0, :]
    with Stage(nc) as S:
        made, turned, copied, stored, own = (S.sem(x) for x in ("rest_made", "turned", "copied", "stored", "own"))
        block = S.block()

        @block.vector
        def _(dve):
            with dve.If(crowded > 0):
                o = Own(dve, own)
                o.seal(nc.vector.tensor_scalar(rest, K.places[:, :, 0:NE], float(SEATS), None, ALU.is_ge))
                nc.vector.tensor_tensor(rest, rest, K.gates[:, :, 0:NE], ALU.mult).then_inc(made, 1)

        @block.tensor
        def _(pe):
            with pe.If(crowded > 0):
                pe.wait_ge(made, 1)
                for t in range(TT):
                    mm = nc.tensor.transpose(K.ps[0:NE, 0, t * P:(t + 1) * P], rest[:, t, :], K.ident[:, :])
                mm.then_inc(turned, 1)

        @block.scalar
        def _(act):
            with act.If(crowded > 0):
                act.wait_ge(turned, 1)
                nc.scalar.activation(rows, K.ps[0:NE, 0, :], ACT.Copy).then_inc(copied, 1)

        @block.sync
        def _(sp):
            with sp.If(crowded > 0):
                sp.wait_ge(copied, 1)
                sp.dma_start(K.ins["gates"], rows).then_inc(stored, 16)
                sp.wait_ge(stored, 16)
    all_tokens_experts(K, crowded, NE, *pick)


def hier_moe(K, l):
    route_groups(K, l)
    token_form(K)
    pick = [lambda i, b, name=name: K.ins[name][l][bass.ds(i * 2 + b, 1)].rearrange("a d f -> (a d) f")
            for name in ("moe_wgate", "moe_wup", "moe_wdown")]
    experts(K, NE // 2, 1, *[lambda i, b, part, of=of: of(i, b) for of in pick])
    seatless(K, pick)



S_KA, S_VN, S_Q, S_GA, S_WK = 3, 4, 5, 6, 7


def shared_kv(K):
    nc = K.nc
    scale_shift(K, K.slot(S_X), K.slot(S_H), lambda k: K.modkv[:, 8 + k:9 + k], lambda k: K.modkv[:, k:k + 1])
    W = K.ins["kv_w"]
    linear(K, W[:, 0:D], D, K.slot(S_H), to_slot(nc, K.slot(S_KA)), wslot=9)
    normalise(K, K.slot(S_KA), K.slot(S_KA), K.slot(S_Q), K.blk[:, :], 1.0 / HD, K.v("eps_rms"), False,
              lambda k: K.v("knorm"), None, per_tile=True)
    h, vn = K.slot(S_H), K.arena[:, S_VN, :].rearrange("p (t d) -> p t d", t=TT)
    wb = [K.slot(9 + b) for b in range(2)]
    wf = K.small[:, 0:KT * HEADS].rearrange("p (k n) -> p k n", n=HEADS)
    one, lf, tmp = (K.flat(64 + j, T)[0:HEADS, :] for j in range(3))
    fb = K.small[0:HEADS, 128:129]
    with Stage(nc) as S:
        w_in, ready, taken, own_d, ex = S.sems("w_in", 3), S.sem("ready"), S.sem("taken"), S.sem("own"), S.sem("exps")
        absd = S.sem("abs_made")
        block = S.block()

        @block.sync
        def _(sp):
            for b in range(2):
                sp.dma_start(wb[b], W[:, D + b * 512:D + (b + 1) * 512].rearrange("(k p) n -> p k n", p=P)).then_inc(w_in[b], 16)
            sp.dma_start(wf, W[:, 2 * D:2 * D + HEADS].rearrange("(k p) n -> p k n", p=P)).then_inc(w_in[2], 16)
            sp.dma_start(fb, K.ins["kv_fb"].rearrange("(p a) -> p a", a=1)).then_inc(w_in[2], 16)

        @block.tensor
        def _(pe):
            pe.wait_ge(w_in[2], 32)
            for k in range(KT):
                mm = nc.tensor.matmul(K.ps[0:HEADS, 7, :], wf[:, k, :], h[:, k, :], start=(k == 0), stop=(k == KT - 1))
            mm.then_inc(ready, 1)
            for b in range(2):
                pe.wait_ge(w_in[b], 16)
                for t in range(TT):
                    if b:
                        pe.wait_ge(taken, t + 1)
                    for k in range(KT):
                        mm = nc.tensor.matmul(K.ps[:, t, :], h[:, k, t * P:(t + 1) * P], wb[b][:, k, :], start=(k == 0), stop=(k == KT - 1))
                    mm.then_inc(ready, 1)

        @block.vector
        def _(dve):
            o = Own(dve, own_d)
            v = nc.vector
            o.seal(v.memset(one, 1.0))
            dve.wait_ge(w_in[2], 32)
            dve.wait_ge(ready, 1)
            o.seal(v.tensor_scalar(lf, K.ps[0:HEADS, 7, :], fb, None, ALU.add))
            o.seal(v.tensor_scalar(tmp, lf, -1.0, None, ALU.mult))
            v.tensor_tensor(tmp, tmp, lf, ALU.max).then_inc(absd, 1)
            dve.wait_ge(ex, 2)
            o.seal(v.scalar_tensor_tensor(out=lf, in0=lf, scalar=0.0, in1=tmp, op0=ALU.min, op1=ALU.subtract))
            o.seal(v.tensor_tensor_scan(K.flat(67, T)[0:HEADS, :], one, lf, 0.0, ALU.mult, ALU.add))

        @block.scalar
        def _(act):
            act.wait_ge(absd, 1)
            nc.scalar.activation(tmp, tmp, ACT.Exp, scale=-1.0).then_inc(ex, 1)
            act.wait_ge(ex, 1)
            nc.scalar.activation(tmp, tmp, ACT.Ln, bias=K.ones[0:HEADS, 0:1]).then_inc(ex, 1)
            for b in range(2):
                for t in range(TT):
                    act.wait_ge(ready, 2 + b * TT + t)
                    nc.scalar.activation(vn[:, t, b * 512:(b + 1) * 512], K.ps[:, t, :], ACT.Copy).then_inc(taken, 1)


def attention(K):
    nc = K.nc
    q, k, out = K.slot(S_Q), K.slot(S_KA), K.slot(2)
    vn = K.arena[:, S_VN, :].rearrange("p (t d) -> p t d", t=TT)
    fc = K.flat(67, T)[0:HEADS, :]
    pb, ptb = K.at(70, 2), K.at(72, 2)
    causal = K.flat(74, P)
    minus = K.small[0:HEADS, 0:HEADS]
    mx, sm, rc = (K.small[:, 32 + 8 * j:34 + 8 * j] for j in range(3))
    rounds = [(h, i) for h in range(HEADS) for i in range(TT)]
    N = len(rounds)
    with Stage(nc) as S:
        loaded, scored, masked, maxd, negd, expd, summed, scaled, turned, copied, mixd, taken = (S.sem(x) for x in (
            "loaded", "scores", "masked", "maxima", "minus_maxima", "exps", "reciprocals", "probs", "probs_turned",
            "probs_copied", "outs", "outs_taken"))
        block = S.block()

        @block.sync
        def _(sp):
            sp.dma_start(causal, K.ins["c_causal"]).then_inc(loaded, 16)
            sp.dma_start(minus, K.ins["c_minus"]).then_inc(loaded, 16)

        def where(n):
            h, i = rounds[n]
            return h, i, slice(64 * (h % 2), 64 * (h % 2) + 64), (i + 1) * P, n % 2

        scores = lambda n: K.ps[:, (0, 1, 6, 7)[n % 4], :]

        @block.tensor
        def _(pe):
            def score(n):
                h, i, f, hi, b = where(n)
                if n >= 4:
                    pe.wait_ge(expd, n - 3)
                nc.tensor.matmul(scores(n)[:, 0:hi], q[f, h // 2, i * P:hi], k[f, h // 2, 0:hi], start=True, stop=False)
                nc.tensor.matmul(scores(n)[:, 0:hi], bc(minus[:, h:h + 1], [HEADS, P]), fc[:, 0:hi], start=False,
                                 stop=True).then_inc(scored, 1)

            def mix(n):
                h, i, f, hi, b = where(n)
                pe.wait_ge(copied, n + 1)
                if n >= 2:
                    pe.wait_ge(taken, n - 1)
                for j in range(i + 1):
                    mm = nc.tensor.matmul(K.ps[f, 4 + b, 0:P], vn[:, j, h * HD:(h + 1) * HD], ptb[:, b, j * P:(j + 1) * P],
                                          start=(j == 0), stop=(j == i))
                mm.then_inc(mixd, 1)

            pe.wait_ge(loaded, 32)
            score(0)
            score(1)
            for n in range(N):
                if n + 2 < N:
                    score(n + 2)
                h, i, f, hi, b = where(n)
                pe.wait_ge(scaled, n + 1)
                if n >= 2:
                    pe.wait_ge(copied, n - 1)
                for j in range(i + 1):
                    mm = nc.tensor.transpose(K.ps[:, 2 + b, j * P:(j + 1) * P], pb[:, b, j * P:(j + 1) * P], K.ident[:, :])
                mm.then_inc(turned, 1)
                if n:
                    mix(n - 1)
            mix(N - 1)

        @block.vector
        def _(dve):
            def maxima(n):
                h, i, f, hi, b = where(n)
                dve.wait_ge(scored, n + 1)
                d = scores(n)[:, i * P:hi]
                nc.vector.tensor_tensor(d, d, causal, ALU.add).then_inc(masked, 1)
                dve.wait_ge(masked, n + 1)
                nc.vector.tensor_reduce(mx[:, b:b + 1], scores(n)[:, 0:hi], AX.X, ALU.max).then_inc(maxd, 1)
                dve.wait_ge(maxd, n + 1)
                nc.vector.tensor_scalar(mx[:, b:b + 1], mx[:, b:b + 1], -1.0, None, ALU.mult).then_inc(negd, 1)

            def take_out(n):
                h, i, f, hi, b = where(n)
                dve.wait_ge(mixd, n + 1)
                nc.vector.tensor_copy(out[f, h // 2, i * P:hi], K.ps[f, 4 + b, 0:P]).then_inc(taken, 1)

            dve.wait_ge(loaded, 32)
            maxima(0)
            for n in range(N):
                h, i, f, hi, b = where(n)
                if n + 1 < N:
                    maxima(n + 1)
                dve.wait_ge(expd, n + 1)
                nc.vector.reciprocal(rc[:, b:b + 1], sm[:, b:b + 1]).then_inc(summed, 1)
                dve.wait_ge(summed, n + 1)
                nc.vector.tensor_scalar(pb[:, b, 0:hi], pb[:, b, 0:hi], rc[:, b:b + 1], None, ALU.mult).then_inc(scaled, 1)
                if n >= 2:
                    take_out(n - 2)
            take_out(N - 2)
            take_out(N - 1)

        @block.scalar
        def _(act):
            for n in range(N + 1):
                if n < N:
                    h, i, f, hi, b = where(n)
                    act.wait_ge(negd, n + 1)
                    if n >= 2:
                        act.wait_ge(turned, n - 1)
                    nc.scalar.activation(pb[:, b, 0:hi], scores(n)[:, 0:hi], ACT.Exp, bias=mx[:, b:b + 1],
                                         accum_out=sm[:, b:b + 1]).then_inc(expd, 1)
                if n:
                    h, i, f, hi, b = where(n - 1)
                    act.wait_ge(turned, n)
                    if n >= 3:
                        act.wait_ge(mixd, n - 2)
                    nc.scalar.activation(ptb[:, b, 0:hi], K.ps[:, 2 + b, 0:hi], ACT.Copy).then_inc(copied, 1)


def fox_layer(K):
    nc = K.nc
    mod = K.mod[1]
    scale_shift(K, K.slot(S_X), K.slot(S_H), lambda k: mod[:, 8 + k:9 + k], lambda k: mod[:, k:k + 1])
    W = K.ins["fx_wqg"][0]
    linear(K, W[:, 0:D], D, K.slot(S_H), to_slot(nc, K.slot(S_Q)), wslot=9)
    linear(K, W[:, D:2 * D], D, K.slot(S_H), to_slot(nc, K.slot(S_GA), ACT.Sigmoid), wslot=9)
    normalise(K, K.slot(S_Q), K.slot(S_Q), K.slot(2), K.blk[:, :], 1.0 / HD, K.v("eps_rms"), False,
              lambda k: K.v("qnorm8"), None, per_tile=True)
    attention(K)
    o = K.slot(2)
    vector_stage(K, lambda dve, own: own.seal(nc.vector.tensor_tensor(o, o, K.slot(S_GA), ALU.mult)))
    linear(K, K.ins["fx_wo"][0], D, o, to_slot(nc, K.slot(5)), wslot=9)


def first_block(K):
    nc = K.nc
    ins = K.ins
    for l in range(DEPTH):
        modulation(K, ins["ada_w"][l], 6 * D, 0, 1, K.vs("ada_b")[:, 48 * l:48 * l + 48], K.mod[l], (8, 16, 32, 40))
    modulation(K, ins["kv_ada_w"], 2 * D, 0, 1, K.vs("kv_ada_b"), K.modkv, (8,))
    modulation(K, ins["w_mod_2"][0], 6 * D, 1, 2, K.vs("b_mod"), K.mod2, (8, 32))
    X = K.slot(S_X)

    def norm_after(l, j, y, at):
        gate = 40 if j else 16
        residual(K, y, lambda k: K.mod[l][:, gate + k:gate + k + 1], X, K.slot(at))
        layer_norm(K, l, j, K.slot(at), K.slot(at + 1), X)

    for l in range(DEPTH):
        if l == 0:
            rwkv_layer(K)
            norm_after(l, 0, K.slot(S_R), 3)
        else:
            fox_layer(K)
            norm_after(l, 0, K.slot(5), 6)
        mod = K.mod[l]
        scale_shift(K, X, K.slot(S_H), lambda k: mod[:, 32 + k:33 + k], lambda k: mod[:, 24 + k:25 + k])
        hier_moe(K, l)
        norm_after(l, 1, K.slot(2), 3)
        if l == 0:
            shared_kv(K)



A_M, A_Y, A_BC, A_XN, A_BN, A_HP, A_WK = 16, 24, 36, 44, 56, 60, 84
C_F, C_Z, C_XBC, C_DT = 0, FW, FW + DI, FW + DI + XBC
C_GATE = C_DT + 2 * SSD_H
HG = SSD_H // SSD_G
GW = HG * HD


def rms_modulate(K, x, dst, tmp, gain, scale, shift, tok=T):
    gs = K.small[:, 2552:2560]
    vector_stage(K, lambda dve, o: o.seal(K.nc.vector.tensor_tensor(gs, gain, scale, ALU.mult)))
    normalise(K, x, dst, tmp, K.mean[:, :], 1.0, K.v("eps_rms"), False, lambda k: gs[:, k:k + 1],
              shift, tok=tok, keep=K.at(88, KT, tok))


def dt_stage(K, h, tok, dtn, acum, wend, total):
    nc = K.nc
    v = nc.vector
    n = tok // P
    H2 = 2 * SSD_H
    wd = K.at(A_WK, 1)[:, 0, 0:KT * H2].rearrange("p (k n) -> p k n", n=H2)
    wk = K.flat(A_WK + 1, 2048)
    bias, al = wk[:, 0:H2], wk[:, H2:2 * H2]
    tri = wk[:, 128:384].rearrange("p (d t) -> p d t", d=2)
    x, da = wk[:, 384:384 + n * H2].rearrange("p (c n) -> p c n", n=H2), K.da[:, 0:n, :]
    ab = wk[:, 768:768 + n * H2].rearrange("p (c n) -> p c n", n=H2)
    flat = lambda bank: K.ps[:, bank, 0:n * H2].rearrange("p (c n) -> p c n", n=H2)
    with Stage(nc) as S:
        loaded, raw, absd, ex, summed, cum, expd, own, al_e = (S.sem(y) for y in (
            "loaded", "raw", "abs_made", "exps", "steps_made", "sums", "end_exps", "own", "rates"))
        block = S.block()

        @block.sync
        def _(sp):
            sp.dma_start(wd, K.ins["w_in_2"][0][:, C_DT:C_GATE].rearrange("(k p) n -> p k n", p=P)).then_inc(loaded, 16)
            sp.dma_start(bias, K.ins["dt_bias_2"].rearrange("a d h -> a (d h)").broadcast_to([P, H2])).then_inc(loaded, 16)
            sp.dma_start(al, K.ins["a_log_2"].rearrange("a d h -> a (d h)").broadcast_to([P, H2])).then_inc(loaded, 16)
            sp.dma_start(tri, K.ins["c_tri"]).then_inc(loaded, 16)

        @block.tensor
        def _(pe):
            pe.wait_ge(loaded, 64)
            for c in range(n):
                for k in range(KT):
                    mm = nc.tensor.matmul(flat(0)[:, c, :], h[:, k, c * P:(c + 1) * P], wd[:, k, :], start=(k == 0), stop=(k == KT - 1))
            mm.then_inc(raw, 1)
            pe.wait_ge(summed, 1)
            for c in range(n):
                for d in range(2):
                    mm = nc.tensor.matmul(flat(1)[:, c, d * SSD_H:(d + 1) * SSD_H], tri[:, d, :],
                                          da[:, c, d * SSD_H:(d + 1) * SSD_H], start=True, stop=True)
            for c in range(n):
                mm = nc.tensor.matmul(flat(2)[:, c, :], K.ones[:, :], da[:, c, :], start=True, stop=True)
            mm.then_inc(cum, 1)

        @block.scalar
        def _(act):
            act.wait_ge(loaded, 64)
            nc.scalar.activation(al, al, ACT.Exp).then_inc(al_e, 1)
            act.wait_ge(absd, 1)
            nc.scalar.activation(ab, ab, ACT.Exp, scale=-1.0).then_inc(ex, 1)
            act.wait_ge(ex, 1)
            nc.scalar.activation(ab, ab, ACT.Ln, bias=K.ones[:, 0:1]).then_inc(ex, 1)
            act.wait_ge(cum, 1)
            nc.scalar.activation(total, flat(2), ACT.Exp).then_inc(expd, 1)
            act.wait_ge(expd, 2)
            nc.scalar.activation(wend, wend, ACT.Exp).then_inc(ex, 1)

        @block.vector
        def _(dve):
            o = Own(dve, own)
            dve.wait_ge(raw, 1)
            o.seal(v.tensor_tensor(x, flat(0), bc(bias.unsqueeze(1), [P, n, H2]), ALU.add))
            o.seal(v.tensor_scalar(ab, x, -1.0, None, ALU.mult))
            v.tensor_tensor(ab, ab, x, ALU.max).then_inc(absd, 1)
            dve.wait_ge(ex, 2)
            o.seal(v.scalar_tensor_tensor(out=dtn, in0=x, scalar=0.0, in1=ab, op0=ALU.max, op1=ALU.add))
            dve.wait_ge(al_e, 1)
            o.seal(v.tensor_scalar(al, al, -1.0, None, ALU.mult))
            v.tensor_tensor(da, dtn, bc(al.unsqueeze(1), [P, n, H2]), ALU.mult).then_inc(summed, 1)
            dve.wait_ge(cum, 1)
            o.seal(v.tensor_copy(acum, flat(1)))
            dve.wait_ge(expd, 1)
            v.tensor_tensor(wend, flat(2), acum, ALU.subtract).then_inc(expd, 1)
            dve.wait_ge(ex, 3)
            o.seal(v.tensor_tensor(wend, wend, dtn, ALU.mult))


def conv_stage(K, raw, tok, row, out_x, out_bc):
    nc = K.nc
    v = nc.vector
    acc = K.at(A_WK, 4, tok)
    with Stage(nc) as S:
        summed, taken, own = S.sem("summed"), S.sem("taken"), S.sem("own")
        block = S.block()

        @block.vector
        def _(dve):
            o = Own(dve, own)
            for t in range(XT):
                u, a = raw[:, t, :], acc[:, t % 4, :]
                rows = lambda s: s.rearrange("p (r w) -> p r w", w=row)
                if t >= 4:
                    dve.wait_ge(taken, t - 3)
                o.seal(v.tensor_scalar(a, u, K.v("conv_w", XT + t), K.v("conv_b", t), ALU.mult, ALU.add))
                o.seal(v.scalar_tensor_tensor(out=rows(a)[:, :, 1:], in0=rows(u)[:, :, :row - 1], scalar=K.v("conv_w", t),
                                              in1=rows(a)[:, :, 1:], op0=ALU.mult, op1=ALU.add))
                v.scalar_tensor_tensor(out=rows(a)[:, :, :row - 1], in0=rows(u)[:, :, 1:], scalar=K.v("conv_w", 2 * XT + t),
                                       in1=rows(a)[:, :, :row - 1], op0=ALU.mult, op1=ALU.add).then_inc(summed, 1)

        @block.scalar
        def _(act):
            for t in range(XT):
                act.wait_ge(summed, t + 1)
                dst = out_x[:, t, :] if t < DIT else out_bc[:, t - DIT, :]
                nc.scalar.activation(dst, acc[:, t % 4, :], ACT.Silu).then_inc(taken, 1)


def turn_stage(K, x, b, n, xn, bn):
    nc = K.nc
    parts = [(c, q) for c in range(n) for q in range(4)]
    with Stage(nc) as S:
        turned, taken = S.sem("turned"), S.sem("taken")
        block = S.block()

        @block.tensor
        def _(pe):
            for m, (c, q) in enumerate(parts):
                if m >= 4:
                    pe.wait_ge(taken, m - 3)
                for j in range(4):
                    src = x[:, 4 * q + j, c * P:(c + 1) * P] if q < 3 else b[:, j, c * P:(c + 1) * P]
                    mm = nc.tensor.transpose(K.ps[:, m % 4, j * P:(j + 1) * P], src, K.ident[:, :])
                mm.then_inc(turned, 1)

        @block.scalar
        def _(act):
            for m, (c, q) in enumerate(parts):
                act.wait_ge(turned, m + 1)
                dst = xn[:, c, q * 512:(q + 1) * 512] if q < 3 else bn[:, c, :]
                nc.scalar.activation(dst, K.ps[:, m % 4, :], ACT.Copy).then_inc(taken, 1)


def state_stage(K, xn, bn, wend, total, walks):
    nc = K.nc
    v = nc.vector
    xw = K.at(A_WK, 4)
    rounds = [(w, g) for w in walks for g in range(SSD_G)]
    with Stage(nc) as S:
        made, summed, added, own = S.sem("weighted"), S.sem("summed"), S.sem("added"), S.sem("own")
        block = S.block()

        @block.vector
        def _(dve):
            o = Own(dve, own)

            def weigh(m):
                (d, c, before, after), g = rounds[m]
                if m >= 2:
                    dve.wait_ge(summed, m - 1)
                w = wend[:, c, d * SSD_H + g * HG:d * SSD_H + (g + 1) * HG]
                v.tensor_tensor(xw[:, m % 2, 0:GW].rearrange("p (h i) -> p h i", h=HG),
                                xn[:, c, g * GW:(g + 1) * GW].rearrange("p (h i) -> p h i", h=HG),
                                bc(w.unsqueeze(2), [P, HG, HD]), ALU.mult).then_inc(made, 1)
            weigh(0)
            for m, ((d, c, before, after), g) in enumerate(rounds):
                if m + 1 < len(rounds):
                    weigh(m + 1)
                cols = slice(g * GW, (g + 1) * GW)
                dve.wait_ge(summed, m + 1)
                if before is None:
                    o.seal(v.tensor_copy(after[:, cols], K.ps[:, m % 2, 0:GW]))
                else:
                    tot = total[:, c, d * SSD_H + g * HG:d * SSD_H + (g + 1) * HG]
                    o.seal(v.tensor_tensor(after[:, cols].rearrange("p (h i) -> p h i", h=HG),
                                           before[:, cols].rearrange("p (h i) -> p h i", h=HG),
                                           bc(tot.unsqueeze(2), [P, HG, HD]), ALU.mult))
                    o.seal(v.tensor_tensor(after[:, cols], after[:, cols], K.ps[:, m % 2, 0:GW], ALU.add))
                dve.sem_inc(added, 1)

        @block.tensor
        def _(pe):
            for m, ((d, c, before, after), g) in enumerate(rounds):
                pe.wait_ge(made, m + 1)
                if m >= 2:
                    pe.wait_ge(added, m - 1)
                nc.tensor.matmul(K.ps[:, m % 2, 0:GW], bn[:, c, g * P:(g + 1) * P], xw[:, m % 2, 0:GW],
                                 start=True, stop=True).then_inc(summed, 1)


def output_stage(K, y, bcm, xn, dtn, acum, hp):
    nc = K.nc
    v = nc.vector
    wk = K.flat(A_WK, 12 * T)
    used = [0]

    def take(*shape):
        m = math.prod(shape)
        s = wk[:, used[0]:used[0] + m]
        used[0] += m
        return s.rearrange("p (a b) -> p a b", a=shape[0]) if len(shape) > 1 else s
    W = [take(HG, P) for _ in range(2)]
    CE2 = [[take(HG, P) for _ in range(2)] for _ in range(2)]
    xd = [take(HG, HD) for _ in range(2)]
    cbm = [take(P) for _ in range(2)]
    tri = take(2, P)
    rounds = [(c, g) for c in range(TT) for g in range(SSD_G)]
    with Stage(nc) as S:
        loaded, rows_made, out_made = S.sem("loaded"), S.sem("rows_made"), S.sem("out_made")
        dve_s = Steps(S.sem("dve_steps"), ["cb0", "cb1", "y0", "y1", "y2"] + [f"seg{d}{h}" for d in range(2) for h in range(HG)] + ["xd0", "xd1"]
                      + ["w0", "w1", "ce0", "ce1"], lead=1)
        act_s = Steps(S.sem("act_steps"), ["er0", "er1", "w0", "w1"], lead=1)
        block = S.block()
        heads = lambda s, n=P: s.rearrange("p (h i) -> p h i", h=HG)
        row = lambda d, h: K.ps[:, 1 + 2 * d + h // 4, (h % 4) * P:(h % 4) * P + P]
        rows = [K.ps[:, 1 + 2 * d:3 + 2 * d, :].rearrange("p b t -> p (b t)")[:, 0:HG * P].rearrange("p (h t) -> p h t", h=HG) for d in range(2)]
        cb = K.ps[:, 0, 0:P]

        @block.sync
        def _(sp):
            sp.dma_start(tri, K.ins["c_tri"]).then_inc(loaded, 16)

        @block.tensor
        def _(pe):
            def make_rows(n):
                c, g = rounds[n]
                now = slice(c * P, (c + 1) * P)
                if n:
                    pe.wait_ge(dve_s.sem, dve_s.at("xd0", n - 1))
                    pe.wait_ge(act_s.sem, act_s.at("er1", n - 1))
                nc.tensor.matmul(cb, bcm[:, g, now], bcm[:, SSD_G + g, now], start=True, stop=True)
                for d in range(2):
                    for h in range(HG):
                        a = d * SSD_H + g * HG + h
                        mm = nc.tensor.matmul(row(d, h), bc(K.da[:, c, a:a + 1], [P, P]), tri[:, d, :], start=True, stop=True)
                mm.then_inc(rows_made, 1)

            pe.wait_ge(loaded, 16)
            make_rows(0)
            for n, (c, g) in enumerate(rounds):
                if n + 1 < len(rounds):
                    make_rows(n + 1)
                pe.wait_ge(dve_s.sem, dve_s.at("ce1", n))
                for h in range(HG):
                    f = slice(64 * (h % 2), 64 * (h % 2) + 64)
                    o = K.ps[f, 5, (h // 2) * P:(h // 2) * P + P]
                    for d in range(2):
                        nc.tensor.matmul(o, xd[d][:, h, :], W[d][:, h, :], start=(d == 0), stop=False, skip_group_check=True)
                        st = hp(d, c)[:, (g * HG + h) * HD:(g * HG + h + 1) * HD]
                        mm = nc.tensor.matmul(o, st, CE2[n % 2][d][:, h, :], start=False, stop=(d == 1), skip_group_check=True)
                mm.then_inc(out_made, 1)

        @block.scalar
        def _(act):
            act.sem_inc(act_s.sem, act_s.base)
            for n, (c, g) in enumerate(rounds):
                CE = CE2[n % 2]
                act.wait_ge(rows_made, n + 1)
                if n >= 2:
                    act.wait_ge(out_made, n - 1)
                for d in range(2):
                    nc.scalar.activation(CE[d], rows[d], ACT.Exp).then_inc(act_s.sem, 1)
                for d in range(2):
                    act.wait_ge(dve_s.sem, dve_s.at(f"seg{d}{HG - 1}", n))
                    nc.scalar.activation(W[d], W[d], ACT.Exp).then_inc(act_s.sem, 1)

        @block.vector
        def _(dve):
            dve.sem_inc(dve_s.sem, dve_s.base)
            dve.wait_ge(loaded, 16)

            def take_out(n):
                c, g = rounds[n]
                now = slice(c * P, (c + 1) * P)
                dve.wait_ge(out_made, n + 1)
                for m in range(3):
                    t = 3 * g + m
                    v.scalar_tensor_tensor(out=y[:, t, now], in0=y[:, t, now], scalar=K.v("d_skip", t),
                                           in1=K.ps[:, 5, m * P:(m + 1) * P], op0=ALU.mult, op1=ALU.add).then_inc(dve_s.sem, 1)

            for n, (c, g) in enumerate(rounds):
                now = slice(c * P, (c + 1) * P)
                CE = CE2[n % 2]
                dve.wait_ge(rows_made, n + 1)
                if n:
                    dve.wait_ge(dve_s.sem, dve_s.at("w1", n - 1))
                for d in range(2):
                    v.tensor_tensor(cbm[d], cb, tri[:, d, :], ALU.mult).then_inc(dve_s.sem, 4 if n == 0 and d == 1 else 1)
                if n:
                    take_out(n - 1)
                for d in range(2):
                    dve.wait_ge(act_s.sem, act_s.at(f"er{d}", n))
                    for h in range(HG):
                        a = d * SSD_H + g * HG + h
                        v.tensor_scalar(W[d][:, h, :], row(d, h), acum[:, c, a:a + 1], 0.0, ALU.subtract, ALU.min).then_inc(dve_s.sem, 1)
                for d in range(2):
                    a = d * SSD_H + g * HG
                    v.tensor_tensor(xd[d], heads(xn[:, c, g * GW:(g + 1) * GW]), bc(dtn[:, c, a:a + HG].unsqueeze(2), [P, HG, HD]),
                                    ALU.mult).then_inc(dve_s.sem, 1)
                for d in range(2):
                    dve.wait_ge(act_s.sem, act_s.at(f"w{d}", n))
                    if d == 0:
                        dve.wait_ge(dve_s.sem, dve_s.at("cb1", n))
                    v.tensor_tensor(W[d], W[d], bc(cbm[d].unsqueeze(1), [P, HG, P]), ALU.mult).then_inc(dve_s.sem, 1)
                for d in range(2):
                    v.tensor_tensor(CE[d], CE[d], bc(bcm[:, SSD_G + g, now].unsqueeze(1), [P, HG, P]), ALU.mult).then_inc(dve_s.sem, 1)
            take_out(len(rounds) - 1)


def fourier_branch(K, uf, dst):
    nc = K.nc
    A = K.flat(40, 4096).rearrange("p (g t c) -> p g t c", g=FT, t=TT)
    CT = K.flat(48, 4096).rearrange("p (t j n) -> p t j n", t=TT, j=2)
    CC = K.small[:, 0:2 * P]
    f = K.at(28, FT)
    with Stage(nc) as S:
        loaded, first, taken, second, own = (S.sem(x) for x in ("loaded", "over_features", "taken", "over_tokens", "stored"))
        block = S.block()

        @block.sync
        def _(sp):
            sp.dma_start(CC, K.ins["c_dft_c"]).then_inc(loaded, 16)
            sp.dma_start(CT, K.ins["c_dft_t"].rearrange("(t p) j n -> p t j n", p=P)).then_inc(loaded, 16)

        @block.tensor
        def _(pe):
            pe.wait_ge(loaded, 32)
            n = 0
            for g in range(FT):
                for t in range(TT):
                    if n >= 4:
                        pe.wait_ge(taken, n - 3)
                    nc.tensor.matmul(K.ps[:, n % 4, 0:2 * P], uf[:, g, t * P:(t + 1) * P], CC, start=True, stop=True).then_inc(first, 1)
                    n += 1
            pe.wait_ge(taken, n)
            for g in range(FT):
                for t in range(TT):
                    for j in range(2):
                        mm = nc.tensor.matmul(K.ps[:, 4 + g, :], A[:, g, t, j * P:(j + 1) * P], CT[:, t, j, :],
                                              start=(t == 0 and j == 0), stop=(t == TT - 1 and j == 1))
                mm.then_inc(second, 1)

        @block.scalar
        def _(act):
            n = 0
            for g in range(FT):
                for t in range(TT):
                    act.wait_ge(first, n + 1)
                    nc.scalar.activation(A[:, g, t, :], K.ps[:, n % 4, 0:2 * P], ACT.Copy).then_inc(taken, 1)
                    n += 1
            for g in range(FT):
                act.wait_ge(second, g + 1)
                nc.scalar.activation(f[:, g, :], K.ps[:, 4 + g, :], ACT.Copy).then_inc(own, 1)
    linear(K, K.ins["w_fourier_2"][0], D, f, to_slot(nc, dst), wslot=10, kt=FT)


def token_mixer(K):
    nc = K.nc
    W = K.ins["w_in_2"][0]
    X, H, M = K.slot(S_X), K.slot(S_H), K.at(A_M, KT)
    mod = K.mod2
    n48 = lambda j: K.small[:, 192 * j:192 * j + 192].rearrange("p (c n) -> p c n", n=48)
    dtn, acum, wend, total = (n48(j) for j in range(4))
    K.da = n48(4)
    hp = lambda d, c: K.flat(A_HP + 3 * (4 * d + c), DI)

    Hc = K.at(A_M, KT, CTX)
    raw = K.at(A_HP, XT, CTX)
    ctx = K.at(A_M + 4, KT, CTX)
    with Stage(nc) as S:
        loaded = S.sem("loaded")
        block = S.block()

        @block.sync
        def _(sp):
            sp.dma_start(ctx, K.ins["ctxT"].rearrange("(k p) t -> p k t", p=P)).then_inc(loaded, 16)
            sp.wait_ge(loaded, 16)
    rms_modulate(K, ctx, Hc, K.at(80, KT, CTX), K.vs("mix_pre"), mod[:, 8:16, 1], lambda k: mod[:, k, 1:2], tok=CTX)
    dt_stage(K, Hc, CTX, dtn[:, 0:2], acum[:, 0:2], wend[:, 0:2], total[:, 0:2])
    linear(K, W[:, C_XBC:C_DT], XBC, Hc, to_slot(nc, raw), wslot=10, tok=CTX)
    xc, bcc = K.at(A_Y, DIT, CTX), K.at(A_BC, 8, CTX)
    conv_stage(K, raw, CTX, CTX, xc, bcc)
    xn = K.flat(A_XN, 2 * DI).rearrange("p (c n) -> p c n", c=2)
    bn = K.flat(52, 2 * 512).rearrange("p (c n) -> p c n", c=2)
    turn_stage(K, xc, bcc[:, 0:SSD_G, :], 2, xn, bn)
    tmp = [K.small[:, 1000:1000 + DI], K.flat(A_BN, DI)]
    state_stage(K, xn, bn, wend, total, [(0, 0, None, tmp[0]), (0, 1, tmp[0], tmp[0]), (1, 1, None, tmp[1]), (1, 0, tmp[1], tmp[1])])

    rms_modulate(K, X, H, K.at(80, KT), K.vs("mix_pre"), mod[:, 8:16, 0], lambda k: mod[:, k, 0:1])

    uf = K.at(24, FT)
    linear(K, W[:, 0:FW], FW, H, to_slot(nc, uf), wslot=10)
    fourier_branch(K, uf, M)
    g = K.at(24, KT)
    linear(K, W[:, C_GATE:C_GATE + D], D, H, to_slot(nc, g, ACT.Sigmoid, K.vs("b_gate")[:, 0:KT]), wslot=10)
    vector_stage(K, lambda dve, o: o.seal(nc.vector.tensor_tensor(M, M, g, ALU.mult)))

    dt_stage(K, H, T, dtn, acum, wend, total)
    raw = K.at(A_HP, XT)
    linear(K, W[:, C_XBC:C_DT], XBC, H, to_slot(nc, raw), wslot=10)
    Y, bcm = K.at(A_Y, DIT), K.at(A_BC, 8)
    conv_stage(K, raw, T, ROW, Y, bcm)

    def seed(dve, o):
        o.seal(nc.vector.tensor_copy(hp(0, 0), tmp[0]))
        o.seal(nc.vector.tensor_copy(hp(1, TT - 1), tmp[1]))
    vector_stage(K, seed)

    xn = K.flat(A_XN, TT * DI).rearrange("p (c n) -> p c n", c=TT)
    bn = K.flat(A_BN, TT * 512).rearrange("p (c n) -> p c n", c=TT)
    turn_stage(K, Y, bcm[:, 0:SSD_G, :], TT, xn, bn)
    state_stage(K, xn, bn, wend, total, [(0, c, hp(0, c), hp(0, c + 1)) for c in range(TT - 1)]
                + [(1, c, hp(1, c), hp(1, c - 1)) for c in range(TT - 1, 0, -1)])
    output_stage(K, Y, bcm, xn, dtn, acum, hp)
    z = K.at(A_BC, DIT)
    linear(K, W[:, C_Z:C_XBC], DI, H, to_slot(nc, z, ACT.Silu), wslot=10)
    vector_stage(K, lambda dve, o: o.seal(nc.vector.tensor_tensor(Y, Y, z, ALU.mult)))
    normalise(K, Y, Y, z, K.ones[:, :], 1.0 / DI, K.v("eps_rms"), False, lambda k: K.v("ssd_norm", k), None, kt=DIT)
    s = K.at(84, KT)
    linear(K, K.ins["w_ssd_out_2"][0], D, Y, to_slot(nc, s), wslot=7, kt=DIT)
    linear(K, W[:, C_GATE + D:C_GATE + 2 * D], D, H, to_slot(nc, g, ACT.Sigmoid, K.vs("b_gate")[:, KT:2 * KT]), wslot=5)

    def merge(dve, o):
        o.seal(nc.vector.tensor_tensor(s, s, g, ALU.mult))
        o.seal(nc.vector.tensor_tensor(M, M, s, ALU.add))
    vector_stage(K, merge)
    linear(K, K.ins["w_out_2"][0], D, M, to_slot(nc, K.slot(3)), wslot=10)


def add_normed(K, y, tmp, gain, scale, x):
    nc = K.nc
    gs = K.small[:, 2552:2560]
    vector_stage(K, lambda dve, o: o.seal(nc.vector.tensor_tensor(gs, gain, scale, ALU.mult)))
    normalise(K, y, y, tmp, K.mean[:, :], 1.0, K.v("eps_rms"), False, lambda k: gs[:, k:k + 1], None)
    vector_stage(K, lambda dve, o: o.seal(nc.vector.tensor_tensor(x, x, y, ALU.add)))


def second_block(K):
    X, H = K.slot(S_X), K.slot(S_H)
    mod = K.mod2
    token_mixer(K)
    add_normed(K, K.slot(3), K.slot(4), K.vs("mix_post"), mod[:, 16:24, 0], X)
    rms_modulate(K, X, H, K.at(80, KT), K.vs("ffn_pre"), mod[:, 32:40, 0], lambda k: mod[:, 24 + k, 0:1])
    route_tokens(K)
    ins = K.ins

    def up(name):
        return lambda i, b, part: ins[name][0][bass.ds(i * 2 + b, 1)].rearrange("a d f -> (a d) f")[:, part * DE:(part + 1) * DE]

    def down(i, b, part):
        return ins["w_e_down_2"][0][bass.ds(i * 2 + b, 1)].rearrange("a d f -> (a d) f")[part * DE:(part + 1) * DE, :]
    token_form(K)
    experts(K, NE2 // 2, FF2 // DE, up("w_e_gate_2"), up("w_e_up_2"), down)
    add_normed(K, K.slot(2), K.slot(3), K.vs("ffn_post"), mod[:, 40:48, 0], X)


SCRATCH = {"gates": (NE, T)}
WEIGHTS = ["ada_w", "kv_ada_w", "w_mod_2", "rw_rkv", "rw_w1", "rw_w2", "rw_a1", "rw_a2", "rw_g1", "rw_g2", "rw_wo",
           "kv_w", "kv_fb", "fx_wqg", "fx_wo", "moe_wgrp", "moe_bgrp", "moe_wexp", "moe_bexp", "moe_wgate", "moe_wup",
           "moe_wdown", "w_in_2", "dt_bias_2", "a_log_2", "w_fourier_2", "w_ssd_out_2", "w_out_2", "w_router_2",
           "w_e_gate_2", "w_e_up_2", "w_e_down_2"]


def other_constants(np):
    j = np.arange(P)
    causal = np.where(j[None, :] <= j[:, None], 0.0, -1e30).astype(np.float32)
    tri = np.stack([j[:, None] <= j[None, :], j[:, None] >= j[None, :]], axis=1).astype(np.float32)
    c = 2 * np.pi * np.outer(j, j) / P
    t = np.arange(T)
    a = 2 * np.pi * (np.outer(t, t) % T) / T
    scale = 1 / math.sqrt(T * P)
    head = np.arange(P) // HD
    pick = (np.arange(30)[None, :] - 14 == head[:, None]).astype(np.float32)
    spread = (np.arange(D)[None, :] // HD == np.arange(HEADS)[:, None]).astype(np.float32)
    return {"c_pick": pick, "c_spread": spread, "c_seats": np.tile(np.arange(SEATS, dtype=np.float32), (P, 1)), "c_causal": causal, "c_minus": -np.eye(HEADS, dtype=np.float32), "c_tri": tri,
            "c_dft_c": np.concatenate([np.cos(c), np.sin(c)], axis=1).astype(np.float32) * np.float32(scale),
            "c_dft_t": np.stack([np.cos(a), -np.sin(a)], axis=1).astype(np.float32)}


def program(nc, ins, cols, out, debug):
    Stage.number, Stage.used = 0, []
    with ExitStack() as ctx:
        K = Core(nc, ctx, ins, cols)
        setup(K)
        first_block(K)
        second_block(K)
        with Stage(nc) as S:
            stored = S.sem("stored")
            block = S.block()

            @block.sync
            def _(sp):
                sp.dma_start(out.rearrange("(k p) t -> p k t", p=P), K.slot(S_X)).then_inc(stored, 16)
                sp.wait_ge(stored, 16)



def columns(inputs, np):
    def flat(a):
        a = np.asarray(a).reshape(-1)
        return a.reshape(-1, P).T
    parts = {
        "ada_b": flat(inputs["ada_b"]), "kv_ada_b": flat(inputs["kv_ada_b"]), "b_mod": flat(inputs["b_mod_2"]),
        "ln_g": flat(inputs["ln_g"]), "ln_b": flat(inputs["ln_b"]), "mu": flat(inputs["rw_mu"]),
        "w0": flat(inputs["rw_w0"]), "a0": flat(inputs["rw_a0"]), "kk": flat(inputs["rw_kk"]), "ka": flat(inputs["rw_ka"]),
        "rk": flat(inputs["rw_rk"]), "gn_g": flat(inputs["rw_gn_g"]), "gn_b": flat(inputs["rw_gn_b"]),
        "c": flat(inputs["c"]), "c_2": flat(inputs["c_2"]), "c_ctx_2": flat(inputs["c_ctx_2"]),
        "knorm": flat(np.tile(np.asarray(inputs["kv_knorm"]).reshape(-1), 2)),
        "qnorm": flat(np.tile(np.asarray(inputs["fx_qnorm"]).reshape(-1), 2)),
        "qnorm8": np.zeros((P, 1), np.float32), "places": np.tile(np.arange(8, dtype=np.float32) - 64, (P, 1)),
        "mix_pre": flat(inputs["norm_mix_pre_2"]), "mix_post": flat(inputs["norm_mix_post_2"]),
        "ffn_pre": flat(inputs["norm_ffn_pre_2"]), "ffn_post": flat(inputs["norm_ffn_post_2"]),
        "conv_w": flat(inputs["conv_w_2"]), "conv_b": flat(inputs["conv_b_2"]), "ssd_norm": flat(inputs["ssd_norm_2"]),
        "b_gate": flat(inputs["b_gate_2"]),
        "d_skip": flat(np.repeat(np.asarray(inputs["d_skip_2"]).reshape(-1), HD)),
        "eps_ln": np.full((P, 1), 1e-5, np.float32), "eps_gn": np.full((P, 1), 64e-5, np.float32),
        "eps_rms": np.full((P, 1), 1e-6, np.float32), "zero": np.zeros((P, 1), np.float32),
    }
    cols, at = {}, 0
    for name, a in parts.items():
        cols[name] = (at, a.shape[1])
        at += a.shape[1]
    return np.ascontiguousarray(np.concatenate(list(parts.values()), axis=1)), cols


def kernel(debug=None, **inputs):
    import numpy as np
    import concourse.bacc as _bacc
    from concourse import mybir as _mybir
    from concourse.bass_utils import run_bass_kernel_spmd as _run

    nc = _bacc.Bacc("TRN2", target_bir_lowering=False, num_devices=1)
    arrays, ins = {}, {}

    def give(name, a):
        a = np.ascontiguousarray(a)
        arrays[f"in_{name}"] = a
        ins[name] = nc.dram_tensor(f"in_{name}", a.shape, _mybir.dt.from_np(a.dtype), kind="ExternalInput").ap()

    vecs, cols = columns(inputs, np)
    give("vecs", vecs)
    give("xT", np.asarray(inputs["x"])[0].T)
    give("ctxT", np.asarray(inputs["ctx_2"])[0].T)
    give("c_ident", np.eye(P, dtype=np.float32))
    give("c_blk", np.kron(np.eye(2), np.ones((HD, HD))).astype(np.float32))
    give("c_wkv", wkv_constants(np))
    for name, a in other_constants(np).items():
        give(name, a)
    for name in WEIGHTS:
        give(name, inputs[name])
    for name, shape in SCRATCH.items():
        ins[name] = nc.dram_tensor(name, shape, F32, kind="Internal").ap()
    if debug:
        ins["debug"] = nc.dram_tensor("debug", debug[1], F32, kind="ExternalOutput").ap()
    out = nc.dram_tensor("out", (D, T), F32, kind="ExternalOutput").ap()
    program(nc, ins, cols, out, debug[0] if debug else None)
    r = _run(nc, [arrays], core_ids=[0])
    return np.ascontiguousarray(r.results[0]["out"].T)[None]
```
